# Optimizing a Trainium2 kernel written in Bass

```python
import jax, jax.numpy as jnp
from jax import lax
import numpy as np

D_MODEL = 2048
BATCH = 1
SEQ = 256
DEPTH = 1

CHUNK = 64
PLE_DIM = 256
EPS = 1e-6

ATT_HEAD_DIM = 64
ATT_WIDTH = D_MODEL // 2
ATT_HEADS = ATT_WIDTH // ATT_HEAD_DIM
BAND_CHUNKS = 9
MAX_REL_DIST = 256

GLA_HEADS = 4
GLA_WIDTH = D_MODEL // 2
GLA_DV = GLA_WIDTH // GLA_HEADS
GLA_KEY_WIDTH = GLA_WIDTH // 2
GLA_DK = GLA_KEY_WIDTH // GLA_HEADS
GLA_GATE_RANK = 16
GLA_GATE_TAU = 16.0

MIX_WIDTH = ATT_WIDTH + GLA_WIDTH
IN_SPLITS = (ATT_WIDTH, ATT_WIDTH, ATT_WIDTH,
             GLA_KEY_WIDTH, GLA_KEY_WIDTH,
             GLA_WIDTH, GLA_WIDTH,
             GLA_GATE_RANK)
IN_PROJ_WIDTH = sum(IN_SPLITS)

D_FF = 5632
CONV_WIDTH = 3


def rms_norm(x, w):
    xf = x.astype(jnp.float32)
    y = xf * lax.rsqrt(jnp.mean(xf * xf, axis=-1, keepdims=True) + EPS)
    return (y * w.astype(jnp.float32)).astype(x.dtype)

def split_cols(t, sizes):
    idx = [int(v) for v in np.cumsum(sizes)[:-1]]
    return jnp.split(t, idx, axis=-1)

def rel_pos_bias(table):
    q_idx = jnp.arange(CHUNK) + (BAND_CHUNKS - 1) * CHUNK
    k_idx = jnp.arange(BAND_CHUNKS * CHUNK)
    dist = jnp.clip(q_idx[:, None] - k_idx[None, :], -MAX_REL_DIST, MAX_REL_DIST) + MAX_REL_DIST
    return table[:, dist]

def chunked_band_attention(q, k, v, bias_table):
    B, T, H, hd = q.shape
    nc = T // CHUNK
    pad = (BAND_CHUNKS - 1) * CHUNK
    band = BAND_CHUNKS * CHUNK
    k_pad = jnp.pad(k, ((0, 0), (pad, 0), (0, 0), (0, 0)))
    v_pad = jnp.pad(v, ((0, 0), (pad, 0), (0, 0), (0, 0)))
    bias = rel_pos_bias(bias_table).astype(jnp.float32)[None]
    key_off = jnp.arange(band) - pad
    q_chunks = q.reshape(B, nc, CHUNK, H, hd).transpose(1, 0, 2, 3, 4)
    scale = hd ** -0.5
    neg = jnp.finfo(jnp.float32).min

    def one_chunk(args):
        c, qc = args
        start = c * CHUNK
        kb = lax.dynamic_slice_in_dim(k_pad, start, band, axis=1)
        vb = lax.dynamic_slice_in_dim(v_pad, start, band, axis=1)
        s = jnp.einsum('bqhd,bkhd->bhqk', qc, kb).astype(jnp.float32) * scale + bias
        valid = (start + key_off) >= 0
        s = jnp.where(valid[None, None, None, :], s, neg)
        pr = jax.nn.softmax(s, axis=-1).astype(vb.dtype)
        return jnp.einsum('bhqk,bkhd->bqhd', pr, vb)

    out = lax.map(one_chunk, (jnp.arange(nc), q_chunks))
    return out.transpose(1, 0, 2, 3, 4).reshape(B, T, H * hd)

def gated_linear_attention(q, k, v, log_a):
    B, T, H, dk = q.shape
    dv = v.shape[-1]
    nc = T // CHUNK

    def to_chunks(t):
        return t.reshape(B, nc, CHUNK, H, t.shape[-1]).transpose(0, 1, 3, 2, 4).astype(jnp.float32)

    qc = to_chunks(q) * (dk ** -0.5)
    kc = to_chunks(k)
    vc = to_chunks(v)
    b = jnp.cumsum(to_chunks(log_a), axis=3)
    b_last = b[:, :, :, -1:, :]
    q_dec = qc * jnp.exp(b)
    k_inv = kc * jnp.exp(-b)
    k_to_end = kc * jnp.exp(b_last - b)
    causal = jnp.tril(jnp.ones((CHUNK, CHUNK), dtype=bool))
    attn = jnp.where(causal, jnp.einsum('bnhid,bnhjd->bnhij', q_dec, k_inv), 0.0)
    o_intra = jnp.einsum('bnhij,bnhjv->bnhiv', attn, vc)

    chunk_update = jnp.einsum('bnhjd,bnhjv->bnhdv', k_to_end, vc)
    chunk_decay = jnp.exp(b_last[:, :, :, 0, :])

    def step(S, xs):
        upd, dec = xs
        return dec[..., None] * S + upd, S

    S0 = jnp.zeros((B, H, dk, dv), jnp.float32)
    _, S_prev = lax.scan(step, S0, (chunk_update.transpose(1, 0, 2, 3, 4),
                                    chunk_decay.transpose(1, 0, 2, 3)))
    S_prev = S_prev.transpose(1, 0, 2, 3, 4)
    o_inter = jnp.einsum('bnhid,bnhdv->bnhiv', q_dec, S_prev)
    o = o_intra + o_inter
    return o.transpose(0, 1, 3, 2, 4).reshape(B, T, H, dv)

def causal_depthwise_conv(u, w, bias):
    T = u.shape[1]
    up = jnp.pad(u, ((0, 0), (CONV_WIDTH - 1, 0), (0, 0)))
    y = bias
    for tap in range(CONV_WIDTH):
        y = y + up[:, tap:tap + T] * w[tap]
    return y

def first_inputs(seed: int = 0) -> dict:
    key = jax.random.key(seed)
    ks = jax.random.split(key, 20)
    f32 = jnp.float32

    def nrm(k, shape, scale):
        return jax.random.normal(k, shape, f32) * scale

    def gain(k, shape):
        return 1.0 + 0.05 * jax.random.normal(k, shape, f32)

    return {
        "x": nrm(ks[0], (BATCH, SEQ, D_MODEL), 1.0),
        "p": nrm(ks[1], (DEPTH, BATCH, SEQ, PLE_DIM), 1.0),
        "norm_mix_w": gain(ks[2], (DEPTH, D_MODEL)),
        "w_in": nrm(ks[3], (DEPTH, D_MODEL, IN_PROJ_WIDTH), D_MODEL ** -0.5),
        "att_rel_bias": nrm(ks[4], (DEPTH, ATT_HEADS, 2 * MAX_REL_DIST + 1), 0.3),
        "w_gla_gate_up": nrm(ks[5], (DEPTH, GLA_GATE_RANK, GLA_KEY_WIDTH), GLA_GATE_RANK ** -0.5),
        "b_gla_gate": nrm(ks[6], (DEPTH, GLA_KEY_WIDTH), 0.5),
        "gla_norm_w": gain(ks[7], (DEPTH, GLA_DV)),
        "w_out": nrm(ks[8], (DEPTH, MIX_WIDTH, D_MODEL), MIX_WIDTH ** -0.5),
        "norm_ffn_w": gain(ks[9], (DEPTH, D_MODEL)),
        "w_ffn_up": nrm(ks[10], (DEPTH, D_MODEL, 2 * D_FF), D_MODEL ** -0.5),
        "w_ffn_conv": nrm(ks[11], (DEPTH, CONV_WIDTH, 2 * D_FF), CONV_WIDTH ** -0.5),
        "b_ffn_conv": nrm(ks[12], (DEPTH, 2 * D_FF), 0.02),
        "w_ffn_down": nrm(ks[13], (DEPTH, D_FF, D_MODEL), D_FF ** -0.5),
        "norm_ple_w": gain(ks[14], (DEPTH, D_MODEL)),
        "w_ple_gate": nrm(ks[15], (DEPTH, D_MODEL, D_MODEL), D_MODEL ** -0.5),
        "w_ple_proj": nrm(ks[16], (DEPTH, PLE_DIM, D_MODEL), PLE_DIM ** -0.5),
        "final_norm_w": gain(ks[17], (D_MODEL,)),
    }

def first_block(x, p, norm_mix_w, w_in, att_rel_bias, w_gla_gate_up, b_gla_gate, gla_norm_w,
              w_out, norm_ffn_w, w_ffn_up, w_ffn_conv, b_ffn_conv, w_ffn_down,
              norm_ple_w, w_ple_gate, w_ple_proj, final_norm_w):
    B, T, _ = x.shape
    for i in range(DEPTH):
        h = rms_norm(x, norm_mix_w[i])
        proj = h @ w_in[i]
        q_a, k_a, v_a, q_g, k_g, v_g, r_g, gate_lr = split_cols(proj, IN_SPLITS)

        hs_a = (B, T, ATT_HEADS, ATT_HEAD_DIM)
        y_a = chunked_band_attention(q_a.reshape(hs_a), k_a.reshape(hs_a), v_a.reshape(hs_a),
                                     att_rel_bias[i])

        gate_logit = (gate_lr @ w_gla_gate_up[i] + b_gla_gate[i]).astype(jnp.float32)
        log_a = (jax.nn.log_sigmoid(gate_logit) / GLA_GATE_TAU).reshape(B, T, GLA_HEADS, GLA_DK)
        o_g = gated_linear_attention(q_g.reshape(B, T, GLA_HEADS, GLA_DK),
                                     k_g.reshape(B, T, GLA_HEADS, GLA_DK),
                                     v_g.reshape(B, T, GLA_HEADS, GLA_DV), log_a)
        o_g = rms_norm(o_g.astype(x.dtype), gla_norm_w[i]).reshape(B, T, GLA_WIDTH)
        y_g = o_g * jax.nn.silu(r_g)

        x = x + jnp.concatenate([y_a, y_g], axis=-1) @ w_out[i]

        h = rms_norm(x, norm_ffn_w[i])
        u = causal_depthwise_conv(h @ w_ffn_up[i], w_ffn_conv[i], b_ffn_conv[i])
        u_gate, u_val = jnp.split(u, 2, axis=-1)
        x = x + (jax.nn.gelu(u_gate) * u_val) @ w_ffn_down[i]

        h = rms_norm(x, norm_ple_w[i])
        g = jax.nn.sigmoid(h @ w_ple_gate[i])
        x = x + g * (p[i] @ w_ple_proj[i])
    return rms_norm(x, final_norm_w)


HEAD_DIM = 128
ATTN_HEADS = 8
RET_HEADS = 8
ATTN_WIDTH = ATTN_HEADS * HEAD_DIM
RET_WIDTH = RET_HEADS * HEAD_DIM
MIX_WIDTH_2 = ATTN_WIDTH + RET_WIDTH
IN_COLS = 3 * ATTN_WIDTH + 4 * RET_WIDTH
D_FF_2 = -(-(8 * D_MODEL) // (3 * 256)) * 256
MOBA_BLOCK = 256
MOBA_TOPK = 3
MOBA_Q_CHUNK = 32
RET_CHUNK = 128
ROPE_THETA = 10000.0
RMS_EPS = 1e-6
NEG_INF = -1e30


def rms_norm_2(x, g):
    xf = x.astype(jnp.float32)
    y = xf * lax.rsqrt(jnp.mean(xf * xf, axis=-1, keepdims=True) + RMS_EPS)
    return (y * g.astype(jnp.float32)).astype(x.dtype)

def rotate_half_split(x, pos, inv_freq):
    ang = pos[:, None] * inv_freq[None, :]
    cos = jnp.cos(ang).astype(x.dtype)
    sin = jnp.sin(ang).astype(x.dtype)
    x1, x2 = jnp.split(x, 2, axis=-1)
    return jnp.concatenate([x1 * cos - x2 * sin, x2 * cos + x1 * sin], axis=-1)

def moba_attention(q, k, v):
    B, H, T, d = q.shape
    BS = MOBA_BLOCK
    QC = MOBA_Q_CHUNK
    NB = -(-T // BS)
    Tp = NB * BS
    NC = T // QC
    K_SEL = min(MOBA_TOPK, max(NB - 1, 1))
    scale = 1.0 / np.sqrt(d)

    pad = ((0, 0), (0, 0), (0, Tp - T), (0, 0))
    kb = jnp.pad(k, pad).reshape(B, H, NB, BS, d)
    vb = jnp.pad(v, pad).reshape(B, H, NB, BS, d)

    k_mean = jnp.mean(kb.astype(jnp.float32), axis=3)
    gate = jnp.einsum('bhtd,bhnd->bhtn', q.astype(jnp.float32), k_mean)
    q_block = jnp.arange(T) // BS
    past = jnp.arange(NB)[None, :] < q_block[:, None]
    gate = jnp.where(past[None, None], gate, NEG_INF)
    _, sel_idx = lax.top_k(gate, K_SEL)

    b_idx = jnp.arange(B)[:, None, None, None]
    h_idx = jnp.arange(H)[None, :, None, None]

    def chunk_step(args):
        c, q_c, idx_c = args
        t = c * QC + jnp.arange(QC)
        kg = kb[b_idx, h_idx, idx_c].reshape(B, H, QC, K_SEL * BS, d)
        vg = vb[b_idx, h_idx, idx_c].reshape(B, H, QC, K_SEL * BS, d)
        valid = jnp.arange(K_SEL)[None, :] < (t // BS)[:, None]
        valid = jnp.repeat(valid, BS, axis=1)
        s_sel = jnp.einsum('bhqd,bhqnd->bhqn', q_c, kg).astype(jnp.float32) * scale
        s_sel = jnp.where(valid[None, None], s_sel, NEG_INF)
        b0 = (c * QC) // BS
        k_own = lax.dynamic_index_in_dim(kb, b0, axis=2, keepdims=False)
        v_own = lax.dynamic_index_in_dim(vb, b0, axis=2, keepdims=False)
        key_pos = b0 * BS + jnp.arange(BS)
        causal = key_pos[None, :] <= t[:, None]
        s_own = jnp.einsum('bhqd,bhkd->bhqk', q_c, k_own).astype(jnp.float32) * scale
        s_own = jnp.where(causal[None, None], s_own, NEG_INF)
        probs = jax.nn.softmax(jnp.concatenate([s_sel, s_own], axis=-1), axis=-1)
        p_sel = probs[..., :K_SEL * BS].astype(v.dtype)
        p_own = probs[..., K_SEL * BS:].astype(v.dtype)
        return (jnp.einsum('bhqn,bhqnd->bhqd', p_sel, vg)
                + jnp.einsum('bhqk,bhkd->bhqd', p_own, v_own))

    q_ch = jnp.moveaxis(q.reshape(B, H, NC, QC, d), 2, 0)
    idx_ch = jnp.moveaxis(sel_idx.reshape(B, H, NC, QC, K_SEL), 2, 0)
    out = lax.map(chunk_step, (jnp.arange(NC), q_ch, idx_ch))
    return jnp.moveaxis(out, 0, 2).reshape(B, H, T, d)

def retention_chunkwise(q, k, v):
    B, H, T, d = q.shape
    dv = v.shape[-1]
    C = RET_CHUNK
    N = T // C
    log_g = jnp.log(1.0 - jnp.power(2.0, -5.0 - jnp.arange(H, dtype=jnp.float32)))
    j = jnp.arange(C, dtype=jnp.float32)
    rel = j[:, None] - j[None, :]
    decay = jnp.where(rel >= 0, jnp.exp(log_g[:, None, None] * jnp.maximum(rel, 0.0)), 0.0)

    qc = q.reshape(B, H, N, C, d)
    kc = k.reshape(B, H, N, C, d)
    vc = v.reshape(B, H, N, C, dv)

    s = jnp.einsum('bhncd,bhnmd->bhncm', qc, kc) * decay[None, :, None]
    intra = jnp.einsum('bhncm,bhnme->bhnce', s, vc)

    k_dec = kc * jnp.exp(log_g[:, None] * (C - 1.0 - j)[None, :])[None, :, None, :, None]
    U = jnp.einsum('bhncd,bhnce->nbhde', k_dec, vc)
    g_chunk = jnp.exp(log_g * C)[None, :, None, None]

    def step(S, U_n):
        return g_chunk * S + U_n, S

    _, S_prev = lax.scan(step, jnp.zeros((B, H, d, dv), jnp.float32), U)
    q_dec = qc * jnp.exp(log_g[:, None] * (j + 1.0)[None, :])[None, :, None, :, None]
    cross = jnp.einsum('bhncd,nbhde->bhnce', q_dec, S_prev)
    return (intra + cross).reshape(B, H, T, dv)

def second_inputs(seed: int = 0) -> dict:
    key = jax.random.key(seed)
    ks = jax.random.split(key, 20)
    f32 = jnp.float32
    nrm = lambda k, shape, fan: jax.random.normal(k, shape, f32) * (fan ** -0.5)
    gain = lambda k, shape: 1.0 + 0.05 * jax.random.normal(k, shape, f32)
    return {
        "x": jax.random.normal(ks[0], (BATCH, SEQ, D_MODEL), f32),
        "p": jax.random.normal(ks[1], (DEPTH, BATCH, SEQ, PLE_DIM), f32),
        "g_mix": gain(ks[2], (DEPTH, D_MODEL)),
        "w_in": nrm(ks[3], (DEPTH, D_MODEL, IN_COLS), D_MODEL),
        "q_norm": gain(ks[4], (DEPTH, HEAD_DIM)),
        "k_norm": gain(ks[5], (DEPTH, HEAD_DIM)),
        "g_ret": gain(ks[6], (DEPTH, RET_WIDTH)),
        "w_o": nrm(ks[7], (DEPTH, MIX_WIDTH_2, D_MODEL), MIX_WIDTH_2),
        "g_ffn": gain(ks[8], (DEPTH, D_MODEL)),
        "w_gate": nrm(ks[9], (DEPTH, D_MODEL, D_FF_2), D_MODEL),
        "w_up": nrm(ks[10], (DEPTH, D_MODEL, D_FF_2), D_MODEL),
        "w_down": nrm(ks[11], (DEPTH, D_FF_2, D_MODEL), D_FF_2),
        "g_ple": gain(ks[12], (DEPTH, D_MODEL)),
        "w_ple_gate": nrm(ks[13], (DEPTH, D_MODEL, D_MODEL), D_MODEL),
        "b_ple_gate": 0.01 * jax.random.normal(ks[14], (DEPTH, D_MODEL), f32),
        "w_ple_proj": nrm(ks[15], (DEPTH, PLE_DIM, D_MODEL), PLE_DIM),
    }

def second_block(x, p, g_mix, w_in, q_norm, k_norm, g_ret, w_o, g_ffn, w_gate, w_up,
              w_down, g_ple, w_ple_gate, b_ple_gate, w_ple_proj):
    B, T, _ = x.shape
    pos = jnp.arange(T, dtype=jnp.float32)
    inv_freq_attn = jnp.power(ROPE_THETA, -jnp.arange(0, HEAD_DIM, 2, dtype=jnp.float32) / HEAD_DIM)
    inv_freq_ret = jnp.power(ROPE_THETA, -jnp.linspace(0.0, 1.0, HEAD_DIM // 2, dtype=jnp.float32))
    split_at = np.cumsum([ATTN_WIDTH] * 3 + [RET_WIDTH] * 3).tolist()

    def heads(t, n):
        return t.reshape(B, T, n, HEAD_DIM).transpose(0, 2, 1, 3)

    for i in range(DEPTH):
        h = rms_norm_2(x, g_mix[i])
        z = h @ w_in[i]
        aq, ak, av, rq, rk, rv, rg = jnp.split(z, split_at, axis=-1)

        aq = rotate_half_split(heads(rms_norm_2(aq.reshape(B, T, ATTN_HEADS, HEAD_DIM), q_norm[i]).reshape(B, T, ATTN_WIDTH), ATTN_HEADS), pos, inv_freq_attn)
        ak = rotate_half_split(heads(rms_norm_2(ak.reshape(B, T, ATTN_HEADS, HEAD_DIM), k_norm[i]).reshape(B, T, ATTN_WIDTH), ATTN_HEADS), pos, inv_freq_attn)
        a_out = moba_attention(aq, ak, heads(av, ATTN_HEADS))
        a_out = a_out.transpose(0, 2, 1, 3).reshape(B, T, ATTN_WIDTH)

        rq_h = rotate_half_split(heads(rq, RET_HEADS), pos, inv_freq_ret).astype(jnp.float32)
        rk_h = (rotate_half_split(heads(rk, RET_HEADS), pos, inv_freq_ret).astype(jnp.float32)
                * (HEAD_DIM ** -0.5))
        r = retention_chunkwise(rq_h, rk_h, heads(rv, RET_HEADS).astype(jnp.float32))
        r = r * lax.rsqrt(jnp.mean(r * r, axis=-1, keepdims=True) + RMS_EPS)
        r = r.transpose(0, 2, 1, 3).reshape(B, T, RET_WIDTH) * g_ret[i].astype(jnp.float32)
        r_out = (jax.nn.silu(rg.astype(jnp.float32)) * r).astype(x.dtype)

        x = x + jnp.concatenate([a_out, r_out], axis=-1) @ w_o[i]

        h2 = rms_norm_2(x, g_ffn[i])
        x = x + (jax.nn.silu(h2 @ w_gate[i]) * (h2 @ w_up[i])) @ w_down[i]

        gate = jax.nn.sigmoid(rms_norm_2(x, g_ple[i]) @ w_ple_gate[i] + b_ple_gate[i])
        x = x + (p[i] @ w_ple_proj[i]) * gate
    return x


def setup_inputs(seed=0):
    out = dict(first_inputs(seed))
    for name, value in second_inputs(seed + 1).items():
        if name != "x":
            out[name + "_2"] = value
    return out


def reference(
    x, p, norm_mix_w, w_in, att_rel_bias, w_gla_gate_up, b_gla_gate, gla_norm_w, w_out,
    norm_ffn_w, w_ffn_up, w_ffn_conv, b_ffn_conv, w_ffn_down, norm_ple_w, w_ple_gate,
    w_ple_proj, final_norm_w, p_2, g_mix_2, w_in_2, q_norm_2, k_norm_2, g_ret_2, w_o_2, g_ffn_2,
    w_gate_2, w_up_2, w_down_2, g_ple_2, w_ple_gate_2, b_ple_gate_2, w_ple_proj_2,
):
    x = first_block(
        x, p, norm_mix_w, w_in, att_rel_bias, w_gla_gate_up, b_gla_gate, gla_norm_w, w_out,
        norm_ffn_w, w_ffn_up, w_ffn_conv, b_ffn_conv, w_ffn_down, norm_ple_w, w_ple_gate,
        w_ple_proj, final_norm_w,
    )
    return second_block(
        x, p_2, g_mix_2, w_in_2, q_norm_2, k_norm_2, g_ret_2, w_o_2, g_ffn_2, w_gate_2, w_up_2,
        w_down_2, g_ple_2, w_ple_gate_2, b_ple_gate_2, w_ple_proj_2,
    )


_drawn_inputs = setup_inputs


def setup_inputs(seed=0):
    import zlib

    import numpy as np

    out = dict(_drawn_inputs(seed))
    spreads = {}
    factors = {'b_ffn_conv': 3.295,
     'norm_ple_w': 5.771,
     'q_norm_2': 8.0,
     'k_norm_2': 8.0,
     'g_ret_2': 2.937,
     'g_ple_2': 22.1,
     'b_ple_gate_2': 200.0}
    for name, (base, spread) in spreads.items():
        noise = np.random.default_rng([zlib.crc32(name.encode()), seed]).standard_normal(out[name].shape)
        drawn = base * np.exp(spread * noise) if base else spread * noise
        out[name] = __import__('jax').numpy.asarray(drawn.astype(out[name].dtype))
    for name, factor in factors.items():
        out[name] = (out[name] * factor).astype(out[name].dtype)
    return out
```

```python
from contextlib import ExitStack
from typing import NamedTuple

import numpy as np

import concourse.bass as bass
from concourse import mybir

F32 = mybir.dt.float32
F32R = mybir.dt.float32r
U32 = mybir.dt.uint32
ALU = mybir.AluOpType
ACT = mybir.ActivationFunctionType
AX_X = mybir.AxisListType.X

P = 128
T = 256
M = T // P
D = 2048
DK = D // P
N = 512
NG = D // N
KU = 4
FF = 5632
FT = FF // P
FS = FF // N
PLE = 256
EPS = 1e-6
NEG = -1e30

CH = 64
AH, AHD = 16, 64
REL = 256
GH, GDK, GDV, RANK = 4, 128, 256, 16
AW = GW = D // 2
GKW = GW // 2
TAU = 16.0
HD, H2 = 128, 8

RAW = 4
SPL = 3
TAPS = 3

VEC_ROWS = ["norm_mix_w", "norm_ffn_w", "norm_ple_w", "g_mix_2", "g_ffn_2", "g_ple_2"]


class Unit(NamedTuple):
    src: object
    nk: int
    width: int
    flipped: bool
    act: int
    k0: int
    group: int
    first: bool
    last: bool


class Turn(NamedTuple):
    src: object
    tiles: int
    act: int
    k0: int
    col: object
    ready: tuple


class Own:

    def __init__(self, eng):
        self.eng, self.n, self.last, self.i, self.per = eng, {}, None, None, {}

    def did(self, sem):
        base = self.n[sem.num] = self.n.get(sem.num, 0) + 1
        self.last = (sem, base if self.i is None else self.i * self.per[sem.num] + base)

    def order(self):
        self.eng.wait_ge(*self.last)

    def enter(self, i, per, last):
        self.i, self.per, self.start = i, {s.num: v for s, v in per}, dict(self.n)
        self.last = (last, i * self.per[last.num] + self.n[last.num])

    def leave(self, rounds, last):
        for num, v in self.per.items():
            assert self.n[num] - self.start.get(num, 0) == v, (num, self.n[num], self.start.get(num), v)
            self.n[num] = self.start.get(num, 0) + v * rounds
        self.i = None
        self.last = (last, self.n[last.num])


def shape_constants():
    c = {}
    c["c_ident"] = np.eye(P, dtype=np.float32)
    j, i = np.meshgrid(np.arange(P), np.arange(P), indexing="ij")
    same = (j // CH == i // CH) & (j <= i)
    c["c_cumsum"] = (same / TAU).astype(np.float32)
    c["c_chunk_mask"] = same.astype(np.uint32)
    causal = np.zeros((P, T), np.float32)
    causal[:, P:] = np.where(i <= j, 0.0, NEG)
    c["c_causal"] = causal
    pos = np.arange(T, dtype=np.float32)[:, None]
    half = HD // 2
    for name, freq in (
        ("c_rope_a", np.power(np.float32(10000.0), -np.arange(0, HD, 2, dtype=np.float32) / np.float32(HD))),
        ("c_rope_r", np.power(np.float32(10000.0), -np.linspace(0.0, 1.0, half, dtype=np.float32))),
    ):
        ang = pos * freq[None, :].astype(np.float32)
        cos, sin = np.cos(ang).astype(np.float32), np.sin(ang).astype(np.float32)
        both = np.stack([np.concatenate([cos, cos], 1), np.concatenate([-sin, sin], 1)], 1)
        c[name] = np.ascontiguousarray(both.reshape(M, P, 2, HD).transpose(1, 0, 2, 3))
    log_g = np.log(1.0 - np.power(2.0, -5.0 - np.arange(H2)))
    rel = (i - j)[:, None, :]
    decay = np.where(rel >= 0, np.exp(log_g[None, :, None] * np.maximum(rel, 0)), 0.0)
    c["c_decay"] = (decay * HD ** -0.5).astype(np.float32)
    c["c_q_decay"] = np.exp(log_g[:, None] * (np.arange(P)[None, :] + 1.0)).astype(np.float32).reshape(1, H2 * P)
    c["c_k_decay"] = (np.exp(log_g[None, :] * (P - 1.0 - np.arange(P)[:, None])) * HD ** -0.5).astype(np.float32)
    return c


def build_two_blocks(nc, a, out, x_spill):
    ctx = ExitStack()
    with ctx:
        def sb(name, shape, dt=F32):
            return ctx.enter_context(nc.sbuf_tensor(name, shape, dt))

        def sem(name):
            return ctx.enter_context(nc.semaphore(name))

        raw = sb("raw", [P, RAW, KU * N])
        w_hi = sb("w_hi", [P, SPL, KU * N], F32R)
        w_lo = sb("w_lo", [P, SPL, KU * N], F32R)
        act_hi = [sb(f"act_hi{b}", [P, DK, T], F32R) for b in range(2)]
        act_lo = [sb(f"act_lo{b}", [P, DK, T], F32R) for b in range(2)]
        SC = 14336
        mem = sb("mem", [P, SC])
        ident = sb("ident", [P, P])
        ones = sb("ones", [P, P])
        diag = sb("diag", [P, T])
        r_row = sb("r_row", [P, T])
        vec_cols = sb("vec_cols", [P, 6 * DK])
        conv_cols = sb("conv_cols", [P, TAPS + 1, 2, FT])
        conv_now = sb("conv_now", [P, TAPS + 1, 2, KU])
        stat = sb("stat", [P, 256])

        x_sb = mem[:, 0:M * D].rearrange("p (m n) -> p m n", m=M)

        def view(at, *dims):
            n = int(np.prod(dims))
            assert at + n <= SC
            v = mem[:, at:at + n]
            if len(dims) == 2:
                return v.rearrange("p (a b) -> p a b", a=dims[0])
            if len(dims) == 3:
                return v.rearrange("p (a b c) -> p a b c", a=dims[0], b=dims[1])
            return v

        ssq1 = stat[:, 0:8].rearrange("p (n m) -> p n m", m=M)
        ssq2 = stat[:, 8:16].rearrange("p (n m) -> p n m", m=M)
        mean1, mean2 = stat[:, 16:18], stat[:, 18:20]
        r_col = stat[:, 20:22]
        r_final = stat[:, 22:24]
        half_neg = stat[:, 24:40]
        mx = stat[:, 40:44].rearrange("p (t h) -> p t h", t=M)
        den = stat[:, 44:48].rearrange("p (t h) -> p t h", t=M)
        rden = stat[:, 48:52].rearrange("p (t h) -> p t h", t=M)
        ssh = stat[:, 52:60]
        rr = stat[:, 60:68]
        glr = stat[:, 68:68 + M * RANK].rearrange("p (m r) -> p m r", m=M)
        k_decay = stat[:, 100:108]
        decay_cols = stat[:, 112:128]
        junk_small = stat[:, 128:136]

        acc = ctx.enter_context(nc.psum_tensor("acc", [P, 2, M, N], F32))
        aux = ctx.enter_context(nc.psum_tensor("aux", [P, 4, N], F32))
        aux01 = aux[:, 0:2, :].rearrange("p b n -> p (b n)")
        aux23 = aux[:, 2:4, :].rearrange("p b n -> p (b n)")

        att_q = [view(3072 * h, 4, T) for h in range(2)]
        att_k = [view(3072 * h + 1024, 4, T) for h in range(2)]
        att_v = [view(3072 * h + 2048, M, N) for h in range(2)]
        BIAS = 6144
        bias = [view(BIAS + 512 * b, 2, T) for b in range(2)]
        scores_sb = view(7168, 2, 384)
        probs_t = view(8192, 2, 384)
        gla_q, gla_k = view(9216, GH, T), view(10240, GH, T)
        log_a = view(11264, M, GKW)
        k_end_nat = view(11264, M, GKW)
        e_diff = view(11264, GH, T)
        e_pos, e_neg = view(12288, GH, T), view(13312, GH, T)
        cumsum_m = view(7936, P)
        chunk_mask = view(8960, P)
        up_aug, glr_t = view(10240, GKW), view(10752, T)
        gla_v = view(0, M, GW)
        gla_r = view(3072, M, GW)
        gla_at = view(5120, 2 * GH, P)
        states = view(6144, 3, GH, GDV)
        neg_part = view(12288, M, GKW)
        neg_abs = view(13312, M, GKW)
        up_in = view(4096, KU, T + 2)
        f_gate = view(5248, KU, T)
        f_val = view(6272, KU, T)
        ple_t = view(4096, M, N)
        p_sb = view(7424, M, PLE)
        wf_b = view(8192, D)
        sq_junk = view(10240, N)
        vec_rows = view(4096, P)
        conv_rows = view(4224, TAPS + 1, P)

        raw_in = [sem(f"raw_in{s}") for s in range(RAW)]
        hi_done, lo_done, unit_used = sem("hi_done"), sem("lo_done"), sem("unit_used")
        acc_free = sem("acc_free")
        const_in, x_in, small_in = sem("const_in"), sem("x_in"), sem("small_in")
        vec_in, bias_in = sem("vec_in"), [sem("bias_in0"), sem("bias_in1")]
        cols_full, cols_done = sem("cols_full"), sem("cols_done")
        turn_full, turn_hi, turned = sem("turn_full"), sem("turn_hi"), sem("turned")
        squared = sem("squared")
        vec_step, act_step, pool_step = sem("vec_step"), sem("act_step"), sem("pool_step")
        mean_done, r_done, diag_done, row_full, row_done = (
            sem("mean_done"), sem("r_done"), sem("diag_done"), sem("row_full"), sem("row_done"))
        scores_full, biased, max_done, exp_done, probs_done = (
            sem("scores_full"), sem("biased"), sem("max_done"), sem("exp_done"), sem("probs_done"))
        pt_full, pt_copied, o_full, o_hi, o_done = (
            sem("pt_full"), sem("pt_copied"), sem("o_full"), sem("o_hi"), sem("o_done"))
        state_first, ones_done, gla_in = sem("state_first"), sem("ones_done"), sem("gla_in")
        ple_tab = [sem("ple_tab0"), sem("ple_tab1")]
        conv_a, conv_b, act_f, f_full, f_hi, f_done = (
            sem("conv_a"), sem("conv_b"), sem("act_f"), sem("f_full"), sem("f_hi"), sem("f_done"))
        gate_done, glr_full, glr_copied, logits_full, log_a_done = (
            sem("gate_done"), sem("glr_full"), sem("glr_copied"), sem("logits_full"), sem("log_a_done"))
        neg_abs_done, log_done = sem("neg_abs_done"), sem("log_done")
        b_full, exps_done, diff_done, ediff_done, decayed = (
            sem("b_full"), sem("exps_done"), sem("diff_done"), sem("ediff_done"), sem("decayed"))
        at_full, at_done, kend_copied, upd_full, state_done = (
            sem("at_full"), sem("at_done"), sem("kend_copied"), sem("upd_full"), sem("state_done"))
        og_full, og_sq, og_r, r_silu, yg_done = (
            sem("og_full"), sem("og_sq"), sem("og_r"), sem("r_silu"), sem("yg_done"))
        ple_in, sig_done, x_fresh, x_stored, x_back = (
            [sem("ple_in0"), sem("ple_in1")], sem("sig_done"), sem("x_fresh"), sem("x_stored"), sem("x_back"))
        z_done, z_sq, z_sum, z_r, roped, qk_full, qk_copied = (
            sem("z_done"), sem("z_sq"), sem("z_sum"), sem("z_r"), sem("roped"), sem("qk_full"), sem("qk_copied"))
        s_full, s_decayed, u_full, s_state, ret_full = (
            sem("s_full"), sem("s_decayed"), sem("u_full"), sem("s_state"), sem("ret_full"))
        mix2_in, tab_in, ret_tab_in, out_stored = sem("mix2_in"), sem("tab_in"), sem("ret_tab_in"), sem("out_stored")

        BASE2 = 10752
        half_q = [view(3072 * h, 4, T) for h in range(2)]
        half_k = [view(3072 * h + 1024, 4, T) for h in range(2)]
        half_v = [view(3072 * h + 2048, M, N) for h in range(2)]
        k_dec = [view(3072 * h + 2048, N) for h in range(2)]
        ret_v = [view(12288, M, N), view(7680, M, N)]
        ret_g = [view(13312, M, N), view(8704, M, N)]
        z, z1, z2 = view(7680, M, N), view(8704, M, N), view(9728, M, N)
        decay_m, q_decay = view(6144, 4, P), view(6656, 4, P)
        g_ret = view(7168, N)
        rope = [view(BASE2 + 512 * n, M, 2, HD) for n in range(3)]
        causal = diag
        score_of = lambda p: scores_sb if p < 8 else view(6144, 2, 384)
        probs_of = lambda p: probs_t if p < 8 else view(6912, 2, 384)
        w_row = sb("w_row", [P, 2 * HD])

        def rows(ap, rows_of_units=None):
            return ap.rearrange("(k p) n -> p k n", p=P)

        w_in1, w_out1 = rows(a["w_in"][0]), rows(a["w_out"][0])
        w_up1, w_down1 = rows(a["w_ffn_up"][0]), rows(a["w_ffn_down"][0])
        w_pg1, w_pp1 = rows(a["w_ple_gate"][0]), rows(a["w_ple_proj"][0])
        w_in2, w_out2 = rows(a["w_in_2"][0]), rows(a["w_o_2"][0])
        w_gate2, w_up2, w_down2 = rows(a["w_gate_2"][0]), rows(a["w_up_2"][0]), rows(a["w_down_2"][0])
        w_pg2, w_pp2 = rows(a["w_ple_gate_2"][0]), rows(a["w_ple_proj_2"][0])
        x_dram = a["x"][0].rearrange("(m p) n -> p m n", p=P)
        out_dram = out[0].rearrange("(m p) n -> p m n", p=P)
        spill = x_spill.rearrange("(m p) n -> p m n", p=P)

        units, after = [], {}

        def unit(w, col, width, flipped, act, k0, nk, group, first, last, needs=()):
            units.append((Unit(w[:, k0:k0 + nk, col:col + width], nk, width, flipped, act, k0, group, first, last), needs))

        def whole(w, col, flipped, act, group, needs):
            for q in range(4):
                unit(w, col, N, flipped, act, KU * q, KU, group, q == 0, q == 3, needs(q))

        def then(slot, *task):
            after.setdefault(slot, []).append(task)

        for n, slot in ((0, -1), (1, -1), (2, 0), (3, 1)):
            then(slot, "turn", n)
        then(1, "square_first")
        then(1, "norm_sums", 0)
        then(2, "norm_row", 0)
        xt0 = lambda q: [(turned, q + 1)]
        qc, kc, vc = 0, AW, 2 * AW
        for h in range(2):
            for n, (col, flipped) in enumerate(((qc, True), (kc, True), (vc, False))):
                g = 3 * h + n
                whole(w_in1, col + N * h, flipped, 0, g, xt0)
                dst = (att_q, att_k, att_v)[n][h]
                then(4 * g + 3, "evac_flipped" if flipped else "evac", g, dst)
        unit(w_in1, 3 * AW + 2 * GKW + 2 * GW, RANK, False, 0, 0, DK, 6, True, True)
        then(24, "rank_out", 6)
        then(25, "rank_turn", 6)
        then(26, "gate_logits", 6)
        gc = 3 * AW
        g1 = [(gc, True, gla_q), (gc + GKW, True, gla_k), (gc + 2 * GKW, False, gla_v[:, :, 0:N]),
              (gc + 2 * GKW + N, False, gla_v[:, :, N:2 * N]), (gc + 2 * GKW + GW, False, gla_r[:, :, 0:N]),
              (gc + 2 * GKW + GW + N, False, gla_r[:, :, N:2 * N])]
        for n, (col, flipped, dst) in enumerate(g1):
            whole(w_in1, col, flipped, 0, 7 + n, xt0)
            then(28 + 4 * n, "evac_flipped" if flipped else "evac", 7 + n, dst)
        then(44, "r_gate", 0)
        then(48, "r_gate", 1)
        for h in range(2):
            for j in range(4):
                at = 12 + 12 * h + 3 * j
                p = 4 * h + j
                then(at, "scores", p)
                then(at + 1, "normalise", p)
                then(at + 2, "probs_turn", p)
                then(at + 3, "weigh", p)
        for slot, task in ((37, "gate_sums"), (39, "gla_scores"), (41, "gla_update01"), (43, "gla_update2"),
                           (44, "gla_out0"), (46, "gla_out1"), (48, "gla_norm")):
            then(slot, task)
        for slot in after:
            after[slot].sort(key=lambda task: {"evac": 0, "evac_flipped": 0, "weigh": 1}.get(task[0], 2))

        u = len(units)
        W1 = u
        assert u == 49
        yt0 = lambda q: [(o_done, 4), (o_done, 8), (turned, 5), (turned, 6)][q:q + 1]
        for n, qs in ((0, (0, 1)), (1, (0, 1)), (0, (2, 3)), (1, (2, 3)), (2, range(4)), (3, range(4))):
            for q in qs:
                unit(w_out1, N * n, N, False, 1, KU * q, KU, 13 + n, q == 0, q == 3, yt0(q))
        then(u + 1, "turn", 4)
        then(u + 2, "turn", 5)
        for n, at in enumerate((5, 7, 11, 15)):
            then(u + at, "residual", 13 + n, n, 0)
            then(u + at, "square_x", 13 + n, n)
            then(u + at + 2, "turn", 6 + n)
        then(u + 16, "norm_sums", 1)
        then(u + 17, "norm_row", 1)
        F1 = len(units)
        units += [None] * (12 * FS)
        G_F1 = 17
        E1 = len(units) - 4
        GD1 = G_F1 + 2 + 6 * (FS - 1)
        for n in range(NG):
            then(E1 + n, "residual", GD1 + n, n, 1)
            then(E1 + n, "square_x", GD1 + n, n)
            then(E1 + n + 2, "turn", 11 + n)
        then(E1 + 1, "turn", 10)
        then(E1 + 4, "norm_sums", 2)

        def embedding(w_gate, w_proj, group, act, p_act, p_k0, turn0, p_turn, block):
            u = len(units)
            for n in range(NG):
                g = group + 2 * n
                whole(w_gate, N * n, False, act, g, lambda q: [(turned, turn0 + q + 1)])
                units.append((Unit(w_proj[:, :, N * n:N * n + N], 2, N, False, p_act, p_k0, g + 1, True, True),
                              [(turned, p_turn + 1)]))
                then(u + 5 * n + 3, "ple_gate", g, n, block)
                then(u + 5 * n + 4, "ple_add", g + 1, n, block)
                if block == 0:
                    then(u + 5 * n + 6, "turn", 15 + n)

        PL1 = len(units)
        G_P1 = GD1 + 4
        embedding(w_pg1, w_pp1, G_P1, 0, 1, DK - 2, 11, 10, 0)
        W2 = len(units)
        then(W2, "final_sums")
        G_W2 = G_P1 + 8
        xt1 = lambda q: [(turned, 15 + q + 1)]
        order = ["aq0", "ak0", "av0", "aq1", "ak1", "av1", "rq0", "rk0", "rv0", "rg0", "rq1", "rk1", "rv1", "rg1"]
        cols = {n: i * 2 * N for i, n in enumerate(("aq", "ak", "av", "rq", "rk", "rv", "rg"))}
        qk = 0
        for i, name in enumerate(order):
            kind, h, g, s = name[:2], int(name[2]), G_W2 + i, W2 + 4 * i + 3
            whole(w_in2, cols[kind] + N * h, False, 1, g, xt1)
            if kind in ("aq", "ak", "rq", "rk"):
                dst = (half_q if kind[1] == "q" else half_k)[h]
                then(s, "rope", g, qk, kind, h)
                then(s + 2, "qk_turn", qk, dst)
                qk += 1
            elif kind == "rg":
                then(s, "evac", g, ret_g[h])
                then(s, "ret_gate", h)
            else:
                then(s, "evac", g, (half_v if kind == "av" else ret_v)[h])
        for p in range(8, 12):
            at = W2 + 12 + 12 * ((p - 8) // 2) + 3 * ((p - 8) % 2)
            then(at, "scores", p)
            then(at + 1, "normalise", p)
            then(at + 2, "probs_turn", p)
            then(at + 3, "weigh", p)
        for h, at in ((0, 40), (1, 56)):
            then(W2 + at, "ret_scores", h)
            then(W2 + at + 1 + (h == 0), "ret_out", h)
            then(W2 + at + 3 + (h == 0), "turn", 19 + h)
        WO2 = len(units)
        G_O2 = G_W2 + 14
        yt1 = lambda q: [(o_done, 10), (o_done, 12), (turned, 20), (turned, 21)][q:q + 1]
        for n, qs in ((0, range(3)), (1, range(3)), (0, (3,)), (1, (3,)), (2, range(4)), (3, range(4))):
            for q in qs:
                unit(w_out2, N * n, N, False, 0, KU * q, KU, G_O2 + n, q == 0, q == 3, yt1(q))
        for n, at in enumerate((6, 7, 11, 15)):
            then(WO2 + at, "residual", G_O2 + n, n, 2)
            then(WO2 + at, "square_x", G_O2 + n, n)
            then(WO2 + at + 2, "turn", 21 + n)
        then(WO2 + 16, "norm_sums", 4)
        then(WO2 + 17, "norm_row", 4)
        F2 = len(units)
        units += [None] * (12 * FS)
        G_F2 = G_O2 + 4
        E2 = len(units) - 4
        GD2 = G_F2 + 2 + 6 * (FS - 1)
        for n in range(NG):
            then(E2 + n, "residual", GD2 + n, n, 1)
            then(E2 + n, "square_x", GD2 + n, n)
            then(E2 + n + 2, "turn", 26 + n)
        then(E2 + 1, "turn", 25)
        then(E2 + 4, "norm_sums", 5)
        PL2 = len(units)
        G_P2 = GD2 + 4
        embedding(w_pg2, w_pp2, G_P2, 1, 0, DK - 2, 26, 25, 1)
        UNITS = len(units)

        col_of = lambda name, n: vec_cols[:, DK * VEC_ROWS.index(name) + 4 * n:DK * VEC_ROWS.index(name) + 4 * n + 4]
        xc = lambda n: x_sb[:, :, N * n:N * n + N]
        turns = [Turn(xc(n), 4, 0, 4 * n, col_of("norm_mix_w", n), (x_in, 16)) for n in range(4)]
        turns += [Turn(gla_r[:, :, N * n:N * n + N], 4, 1, 8 + 4 * n, None, (yg_done, 1)) for n in range(2)]
        turns += [Turn(xc(n), 4, 0, 4 * n, col_of("norm_ffn_w", n), (acc_free, 14 + n)) for n in range(4)]
        turns += [Turn(p_sb, 2, 1, DK - 2, None, (ple_in[0], 16))]
        turns += [Turn(xc(n), 4, 0, 4 * n, col_of("norm_ple_w", n), (acc_free, GD1 + 1 + n)) for n in range(4)]
        turns += [Turn(xc(n), 4, 1, 4 * n, col_of("g_mix_2", n), (x_fresh, 2 * n + 2)) for n in range(4)]
        turns += [Turn(ret_g[h], 4, 0, 8 + 4 * h, None, (yg_done, 2 + h)) for h in range(2)]
        turns += [Turn(xc(n), 4, 1, 4 * n, col_of("g_ffn_2", n), (acc_free, G_O2 + 1 + n)) for n in range(4)]
        turns += [Turn(p_sb, 2, 0, DK - 2, None, (ple_in[1], 16))]
        turns += [Turn(xc(n), 4, 1, 4 * n, col_of("g_ple_2", n), (acc_free, GD2 + 1 + n)) for n in range(4)]
        chunk = lambda t: xc(t)

        def fours(v):
            return v.rearrange("p (f t) -> p f t", f=KU)

        FFN = [
            dict(u=F1, g=G_F1, act=0, f_act=1, it0=0, w=((w_up1, 0), (w_up1, FF)), down=w_down1),
            dict(u=F2, g=G_F2, act=1, f_act=0, it0=FS, w=((w_gate2, 0), (w_up2, 0)), down=w_down2),
        ]

        def ffn_src(b, j, i):
            f = FFN[b]
            if 4 <= j < 8:
                return f["down"][:, bass.ds(KU * i, KU), N * (j - 4):N * (j - 3)]
            w, c = f["w"][0 if j < 4 else 1]
            q = j % 4
            if isinstance(i, int):
                return w[:, KU * q:KU * q + KU, c + N * i:c + N * i + N]
            return w[:, KU * q:KU * q + KU, bass.ds(i * N + c, N)]

        def raw_slot(s, nk, width):
            return raw[:, s, 0:nk * width].rearrange("p (k n) -> p k n", k=nk)

        block = ctx.enter_context(nc.Block())

        @block.sync
        def _(sp):
            sp.dma_start(x_sb, x_dram).then_inc(x_in, 16)
            sp.dma_start(ident[:], a["c_ident"]).then_inc(const_in, 16)
            for r, name in enumerate(VEC_ROWS):
                sp.dma_start(vec_rows[DK * r:DK * r + DK, :],
                             a[name][0].rearrange("(r c) -> r c", c=P)).then_inc(vec_in, 16)
            sp.dma_start(conv_rows[0:2 * FT, 0:TAPS, :],
                         a["w_ffn_conv"][0].rearrange("t (r c) -> r t c", c=P)).then_inc(vec_in, 16)
            sp.dma_start(conv_rows[0:2 * FT, TAPS, :],
                         a["b_ffn_conv"][0].rearrange("(r c) -> r c", c=P)).then_inc(vec_in, 16)

            def load(u, src, nk, width):
                if u >= RAW:
                    sp.wait_ge(lo_done, u - RAW + 1)
                sp.dma_start(raw_slot(u % RAW, nk, width), src).then_inc(raw_in[u % RAW], 16)

            def load_units(lo, hi):
                for u in range(lo, hi):
                    d = units[u][0]
                    load(u, d.src, d.nk, d.width)

            def load_ffn(b):
                u0 = FFN[b]["u"]
                for j in range(8):
                    load(u0 + j, ffn_src(b, j if j < 4 else j + 4, 0), KU, N)
                with sp.Fori(0, FS - 1) as i:
                    for j in range(12):
                        u = u0 + 8 + j
                        sp.wait_ge(lo_done, i * 12 + (u - RAW + 1))
                        src = ffn_src(b, j, i if 4 <= j < 8 else i + 1)
                        sp.dma_start(raw_slot(u % RAW, KU, N), src).then_inc(raw_in[u % RAW], 16)
                for j in range(4, 8):
                    load(u0 + 12 * FS - 8 + j, ffn_src(b, j, FS - 1), KU, N)

            load_units(0, F1)
            load_ffn(0)
            load_units(PL1, F2)
            load_ffn(1)
            load_units(PL2, UNITS)
            sp.wait_ge(out_stored, 16 * NG)

        last_unit = {d.group: u for u, x in enumerate(units) if x for d in x[:1] if d.last}
        last_unit.update({(GD1, GD2)[b] + n: (E1, E2)[b] + n for b in range(2) for n in range(NG)})

        def full(g):
            return last_unit[g] + 1

        def walk(unit_of, tasks, lo, hi):
            for u in range(lo, hi):
                unit_of(u)
                for name, *args in after.get(u, ()):
                    if name in tasks:
                        tasks[name](*args)

        @block.scalar
        def _(act):
            own = Own(act)

            def split(u):
                if u >= UNITS:
                    return
                act.wait_ge(raw_in[u % RAW], 16 * (u // RAW + 1))
                if u >= SPL:
                    act.wait_ge(unit_used, u - SPL + 1)
                act.activation(w_hi[:, u % SPL, :], raw[:, u % RAW, :], ACT.Copy).then_inc(hi_done, 1)

            def split_at(i, u, seam=0):
                act.wait_ge(raw_in[u % RAW], i * 48 + 16 * (u // RAW + 1))
                act.wait_ge(unit_used, i * 12 + (u - SPL + 1))
                act.activation(w_hi[:, u % SPL, :], raw[:, u % RAW, :], ACT.Copy).then_inc(hi_done, 1)

            def step(func, dst, src, sem=act_step, **kw):
                act.activation(dst, src, func, **kw).then_inc(sem, 1)
                own.did(sem)

            def turn(t):
                d = turns[t]
                act.wait_ge(turn_full, t + 1)
                if d.col is None:
                    step(ACT.Copy, act_hi[d.act][:, d.k0:d.k0 + d.tiles, :],
                         aux01[:, 0:T * d.tiles].rearrange("p (f t) -> p f t", f=d.tiles), turn_hi)
                    return
                act.wait_ge(cols_done, 2)
                for k in range(d.tiles):
                    step(ACT.Copy, act_hi[d.act][:, d.k0 + k, :], fours(aux01)[:, k, :],
                         turn_hi if k == d.tiles - 1 else act_step, scale=d.col[:, k:k + 1])

            def square_pair(src, sums):
                for m in range(M):
                    if own.last is not None:
                        own.order()
                    step(ACT.Square, sq_junk, src[:, m, :], squared, accum_out=sums[:, m:m + 1])

            def square_first():
                act.wait_ge(x_in, 16)
                for n in range(NG):
                    square_pair(xc(n), ssq1[:, n, :])

            def square_x(g, n):
                act.wait_ge(acc_free, g + 1)
                square_pair(xc(n), ssq1[:, n, :])

            def scores(p):
                act.wait_ge(max_done, 2 * p + 2)
                own.order()
                for t, lo, hi in ((0, 0, P), (1, P, P + T)):
                    for hh in range(2):
                        step(ACT.Exp, score_of(p)[:, hh, lo:hi], score_of(p)[:, hh, lo:hi], exp_done,
                             bias=mx[:, t, hh:hh + 1], accum_out=den[:, t, hh:hh + 1])

            def probs_turn(p):
                act.wait_ge(pt_full, p + 1)
                own.order()
                step(ACT.Copy, probs_of(p), aux[:, 2:4, 0:384], pt_copied)

            def weigh(p):
                act.wait_ge(o_full, p + 1)
                own.order()
                if p < 8:
                    step(ACT.Copy, act_hi[1][:, p, :], aux[:, 2, 0:T], o_hi)
                else:
                    j = 2 * (p - 8)
                    step(ACT.Copy, act_hi[0][:, j:j + 2, :], aux[:, 2, :].rearrange("p (h t) -> p h t", h=2), o_hi)

            def gate_logits(g):
                act.wait_ge(neg_abs_done, 1)
                own.order()
                step(ACT.Exp, neg_abs, neg_abs)
                own.order()
                step(ACT.Ln, neg_abs, neg_abs, log_done, bias=1.0)

            def gate_sums():
                act.wait_ge(b_full, 1)
                act.wait_ge(diff_done, 1)
                own.order()
                step(ACT.Exp, e_pos, fours(aux01), exps_done)
                step(ACT.Exp, e_neg, fours(aux01), exps_done, scale=-1.0)
                step(ACT.Exp, e_diff, e_diff, ediff_done)

            def gla_scores():
                act.wait_ge(at_full, 1)
                own.order()
                step(ACT.Copy, k_end_nat.rearrange("p m n -> p (m n)"), aux23, kend_copied)

            def gla_update01():
                act.wait_ge(upd_full, 1)
                own.order()
                step(ACT.Copy, states[:, 0, :, :], fours(aux01), state_first)

            def gla_squares(m):
                act.wait_ge(og_full, m + 1)
                for h in range(GH):
                    own.order()
                    step(ACT.Square, e_neg[:, 0, :], fours((aux23, aux01)[m])[:, h, :], og_sq,
                         accum_out=ssh[:, GH * m + h:GH * m + h + 1])

            def r_gate(g):
                act.wait_ge(acc_free, 12 + g)
                own.order()
                step(ACT.Silu, gla_r[:, :, N * g:N * g + N], gla_r[:, :, N * g:N * g + N], r_silu)

            def conv_first(b, it, part, acc_g):
                act.wait_ge(acc_free, acc_g)
                own.order()
                dst = (f_gate, f_val)[part]
                if b == 0:
                    for f in range(KU):
                        step(ACT.Identity, dst[:, f, :], up_in[:, f, TAPS - 1:TAPS - 1 + T], conv_a,
                             scale=conv_now[:, TAPS - 1, part, f:f + 1], bias=conv_now[:, TAPS, part, f:f + 1])
                if part == 0:
                    if b == 0:
                        act.wait_ge(conv_b, it * 8 + 4)
                    own.order()
                    step(ACT.Gelu_apprx_tanh if b == 0 else ACT.Silu, dst, dst, act_f)

            def f_round(b, it):
                f = FFN[b]
                act.wait_ge(f_full, it + (f["it0"] + 1))
                own.order()
                step(ACT.Copy, act_hi[f["f_act"]][:, 0:KU, :], f_val, f_hi)

            def ffn(b):
                f = FFN[b]
                u0, g0 = f["u"], f["g"]
                own.order()
                for j in range(8):
                    split(u0 + j + SPL)
                    for name, *args in after.get(u0 + j, ()):
                        if name in tasks:
                            tasks[name](*args)
                    if j == 3:
                        conv_first(b, 0, 0, g0 + 1)
                    if j == 7:
                        conv_first(b, 0, 1, g0 + 2)
                        f_round(b, 0)
                with act.Fori(0, FS - 1) as i:
                    per = [(act_f, 1), (f_hi, 1)] + [(conv_a, 8)] * (b == 0)
                    own.enter(i, per, f_hi)
                    for j in range(12):
                        split_at(i, u0 + 8 + j + SPL)
                        if j == 3:
                            conv_first(b, i + 1, 0, i * 6 + (g0 + 3))
                        if j == 11:
                            conv_first(b, i + 1, 1, i * 6 + (g0 + 8))
                            f_round(b, i + 1)
                    own.leave(FS - 1, f_hi)

            def ple_gate(g, n, b):
                act.wait_ge(acc_free, g + 1)
                own.order()
                step(ACT.Sigmoid, ple_t, ple_t, sig_done)

            def ple_add(g, n, b):
                if b == 0:
                    act.wait_ge(x_fresh, 2 * n + 1)
                    square_pair(ple_t, ssq1[:, n, :])
                    act.wait_ge(x_fresh, 2 * n + 2)
                    square_pair(xc(n), ssq2[:, n, :])

            def rope_square(g, q, kind, h):
                if kind[0] == "a":
                    act.wait_ge(acc_free, g + 1)
                    own.order()
                    step(ACT.Square, z1, z, z_sq)

            def qk_copy(q, dst):
                if q == 0:
                    act.wait_ge(x_stored, 16 * NG)
                act.wait_ge(qk_full, q + 1)
                own.order()
                step(ACT.Copy, dst, fours(aux01), qk_copied)

            def ret_gate(h):
                act.wait_ge(acc_free, G_W2 + (10, 14)[h])
                own.order()
                step(ACT.Silu, ret_g[h], ret_g[h], r_silu)

            def ret_scores(h):
                act.wait_ge(s_full, h + 1)
                own.order()
                step(ACT.Copy, k_dec[h], aux[:, 2, :], s_state)

            def ret_out(h):
                act.wait_ge(ret_full, h + 1)
                own.order()
                step(ACT.Square, half_k[h], fours(aux23), og_sq)

            tasks = dict(turn=turn, square_first=square_first, square_x=square_x, scores=scores, probs_turn=probs_turn, weigh=weigh,
                         gate_logits=gate_logits, gate_sums=gate_sums, gla_scores=gla_scores,
                         gla_update01=gla_update01, gla_out0=lambda: gla_squares(0), gla_out1=lambda: gla_squares(1),
                         r_gate=r_gate, ple_gate=ple_gate, ple_add=ple_add, rope=rope_square, qk_turn=qk_copy,
                         ret_gate=ret_gate, ret_scores=ret_scores, ret_out=ret_out)
            for u in range(SPL):
                split(u)
            walk(lambda u: split(u + SPL) if u >= 0 else None, tasks, -1, F1)
            ffn(0)
            walk(lambda u: split(u + SPL), tasks, PL1 - 4, F2)
            ffn(1)
            walk(lambda u: split(u + SPL), tasks, PL2 - 4, UNITS)

        @block.vector
        def _(v):
            own = Own(v)

            def remainder(u):
                if u >= UNITS:
                    return
                v.wait_ge(hi_done, u + 1)
                v.tensor_tensor(w_lo[:, u % SPL, :], raw[:, u % RAW, :], w_hi[:, u % SPL, :],
                                ALU.subtract).then_inc(lo_done, 1)

            def remainder_at(i, u):
                v.wait_ge(hi_done, i * 12 + (u + 1))
                v.tensor_tensor(w_lo[:, u % SPL, :], raw[:, u % RAW, :], w_hi[:, u % SPL, :],
                                ALU.subtract).then_inc(lo_done, 1)

            def did(sem=vec_step):
                own.did(sem)

            def turn(t):
                d = turns[t]
                v.wait_ge(turn_hi, t + 1)
                own.order()
                lo, hi = act_lo[d.act], act_hi[d.act]
                if d.col is None:
                    at = slice(d.k0, d.k0 + d.tiles)
                    v.tensor_tensor(lo[:, at, :], aux01[:, 0:T * d.tiles].rearrange("p (f t) -> p f t", f=d.tiles),
                                    hi[:, at, :], ALU.subtract).then_inc(turned, 1)
                    did(turned)
                    return
                for k in range(d.tiles):
                    s = turned if k == d.tiles - 1 else vec_step
                    v.scalar_tensor_tensor(lo[:, d.k0 + k, :], fours(aux01)[:, k, :], d.col[:, k:k + 1],
                                           hi[:, d.k0 + k, :].bitcast(F32), ALU.mult, ALU.subtract).then_inc(s, 1)
                    did(s)

            def norm_sums(k):
                v.wait_ge(squared, (8, 16, 24, 40, 48, 56)[k])
                own.order()
                v.tensor_reduce(mean1, ssq1.rearrange("p n m -> p m n"), AX_X, ALU.add).then_inc(vec_step, 1)
                did()
                own.order()
                v.tensor_scalar(mean1, mean1, 1.0 / D, EPS, ALU.mult, ALU.add).then_inc(mean_done, 1)
                did(mean_done)

            def norm_row(k):
                v.wait_ge(r_done, (1, 2, 3, 4, 5, 6)[k])
                own.order()
                for m in range(M):
                    v.tensor_scalar(diag[:, P * m:P * m + P], ident[:], r_col[:, m:m + 1], None,
                                    ALU.mult).then_inc(diag_done, 1)
                    did(diag_done)
                r = (0, 1, None, None, 2)[k]
                v.wait_ge(row_full, r + 1)
                own.order()
                v.tensor_copy(r_row[:], aux[:, 2, 0:T]).then_inc(row_done, 1)
                did(row_done)
                if k == 1:
                    v.memset(up_in[:, :, 0:TAPS - 1], 0.0).then_inc(vec_step, 1)
                    did()

            def final_sums():
                norm_sums(3)
                own.order()
                v.tensor_reduce(mean2, ssq2.rearrange("p n m -> p m n"), AX_X, ALU.add).then_inc(vec_step, 1)
                did()
                own.order()
                v.tensor_scalar(mean2, mean2, 1.0 / D, None, ALU.mult).then_inc(vec_step, 1)
                did()
                own.order()
                v.scalar_tensor_tensor(mean2, mean1, EPS, mean2, ALU.mult, ALU.add).then_inc(mean_done, 1)
                did(mean_done)

            def evac(g, dst):
                v.wait_ge(unit_used, full(g))
                v.wait_ge(r_done, 1 if g < 13 else 3 if g < G_W2 else 4)
                own.order()
                for m in range(M):
                    s = acc_free if m == M - 1 else vec_step
                    v.tensor_scalar(dst[:, m, :], acc[:, g % 2, m, :], r_col[:, m:m + 1], None,
                                    ALU.mult).then_inc(s, 1)
                    did(s)

            def evac_flipped(g, dst, value=None):
                v.wait_ge(unit_used, full(g) if value is None else value)
                own.order()
                v.tensor_tensor(dst, fours(acc[:, g % 2, :, :].rearrange("p b n -> p (b n)")),
                                r_row[:].unsqueeze(1).to_broadcast([P, KU, T]), ALU.mult).then_inc(acc_free, 1)
                did(acc_free)

            def residual(g, n, how):
                v.wait_ge(unit_used, full(g))
                if how != 1 and n == 0:
                    v.wait_ge(x_back, 16 * (1 + (how == 2)))
                own.order()
                if how < 2:
                    v.tensor_tensor(xc(n), acc[:, g % 2, :, :], xc(n), ALU.add).then_inc(acc_free, 1)
                    did(acc_free)
                    return
                for m in range(M):
                    s = acc_free if m == M - 1 else vec_step
                    v.scalar_tensor_tensor(xc(n)[:, m, :], xc(n)[:, m, :], r_final[:, m:m + 1],
                                           acc[:, g % 2, m, :], ALU.mult, ALU.add).then_inc(s, 1)
                    did(s)

            def scores(p):
                v.wait_ge(scores_full, p + 1)
                if p < 8:
                    b = bias[p % 2]
                    v.wait_ge(bias_in[p % 2], 16 * (p // 2 + 1))
                    own.order()
                    v.memset(b[0:CH, :, 0:CH], NEG).then_inc(vec_step, 1)
                    did()
                    both = (b[:, :, P - 1::-1], b[:, :, T - 1::-1])
                    scale = AHD ** -0.5
                else:
                    v.wait_ge(tab_in, 16 * 6)
                    both = (causal[:, P:T].unsqueeze(1).to_broadcast([P, 2, P]),
                            causal[:].unsqueeze(1).to_broadcast([P, 2, T]))
                    scale = HD ** -0.5
                own.order()
                for t, lo, hi in ((0, 0, P), (1, P, P + T)):
                    v.scalar_tensor_tensor(score_of(p)[:, :, lo:hi], aux[:, 0:2, lo:hi], scale, both[t],
                                           ALU.mult, ALU.add).then_inc(biased, 1)
                    did(biased)
                own.order()
                for t, lo, hi in ((0, 0, P), (1, P, P + T)):
                    v.tensor_reduce(mx[:, t, :], score_of(p)[:, :, lo:hi], AX_X, ALU.max,
                                    negate=True).then_inc(max_done, 1)
                    did(max_done)

            def normalise(p):
                v.wait_ge(exp_done, 4 * p + 4)
                own.order()
                v.reciprocal(rden, den).then_inc(vec_step, 1)
                did()
                own.order()
                for t, lo, hi in ((0, 0, P), (1, P, P + T)):
                    for hh in range(2):
                        v.tensor_scalar(score_of(p)[:, hh, lo:hi], score_of(p)[:, hh, lo:hi], rden[:, t, hh:hh + 1], None,
                                        ALU.mult).then_inc(probs_done, 1)
                        did(probs_done)

            def weigh(p):
                v.wait_ge(o_hi, p + 1)
                own.order()
                if p < 8:
                    dst, src, hi = act_lo[1][:, p, :], aux[:, 2, 0:T], act_hi[1][:, p, :]
                else:
                    j = 2 * (p - 8)
                    dst, hi = act_lo[0][:, j:j + 2, :], act_hi[0][:, j:j + 2, :]
                    src = aux[:, 2, :].rearrange("p (h t) -> p h t", h=2)
                v.tensor_tensor(dst, src, hi, ALU.subtract).then_inc(o_done, 1)
                did(o_done)

            def rank_out(g):
                v.wait_ge(unit_used, full(g))
                own.order()
                v.memset(glr_t[0:RANK + 1, :], 1.0).then_inc(vec_step, 1)
                did()
                for m in range(M):
                    v.tensor_scalar(glr[:, m, :], acc[:, g % 2, m, 0:RANK], r_col[:, m:m + 1], None,
                                    ALU.mult).then_inc(gate_done, 1)
                    did(gate_done)

            def rank_turn(g):
                v.wait_ge(glr_full, 1)
                own.order()
                v.tensor_copy(glr_t[0:RANK, :], acc[0:RANK, g % 2, 0, T:2 * T]).then_inc(glr_copied, 1)
                did(glr_copied)

            def gate_logits(g):
                v.wait_ge(logits_full, 1)
                own.order()
                v.tensor_scalar(neg_part, acc[:, g % 2, :, :], 0.0, None, ALU.min).then_inc(vec_step, 1)
                did()
                v.tensor_scalar(log_a, acc[:, g % 2, :, :], 0.0, None, ALU.max).then_inc(acc_free, 1)
                did(acc_free)
                own.order()
                v.tensor_tensor(neg_abs, neg_part, log_a, ALU.subtract).then_inc(neg_abs_done, 1)
                did(neg_abs_done)
                own.order()
                v.wait_ge(log_done, 1)
                v.tensor_tensor(log_a, neg_part, neg_abs, ALU.subtract).then_inc(log_a_done, 1)
                did(log_a_done)

            def gate_sums():
                v.wait_ge(b_full, 1)
                own.order()
                ends = aux01.rearrange("p (h i) -> p h i", i=CH)[:, :, CH - 1]
                v.tensor_copy(decay_cols, ends).then_inc(vec_step, 1)
                did()
                own.order()
                v.tensor_tensor(e_diff.rearrange("p h (c i) -> p (h c) i", i=CH),
                                decay_cols.unsqueeze(2).to_broadcast([P, 16, CH]),
                                aux01.rearrange("p (h i) -> p h i", i=CH), ALU.subtract).then_inc(diff_done, 1)
                did(diff_done)
                v.wait_ge(exps_done, 2)
                v.scalar_tensor_tensor(gla_q, gla_q, GDK ** -0.5, e_pos, ALU.mult, ALU.mult).then_inc(decayed, 1)
                did(decayed)
                v.tensor_tensor(e_neg, gla_k, e_neg, ALU.mult).then_inc(decayed, 1)
                did(decayed)
                v.wait_ge(ediff_done, 1)
                own.order()
                v.tensor_tensor(gla_k, gla_k, e_diff, ALU.mult).then_inc(decayed, 1)
                did(decayed)

            def gla_scores():
                v.memset(gla_at, 0.0).then_inc(vec_step, 1)
                did()
                v.wait_ge(at_full, 1)
                own.order()
                v.wait_ge(gla_in, 32)
                v.copy_predicated(gla_at, chunk_mask.bitcast(U32).unsqueeze(1).to_broadcast([P, 2 * GH, P]),
                                  aux01.rearrange("p (h i) -> p h i", i=P)).then_inc(at_done, 1)
                did(at_done)

            def carry(c, src):
                for h in range(GH):
                    v.scalar_tensor_tensor(states[:, c, h, :], states[:, c - 1, h, :],
                                           e_pos[:, h, CH * c + CH - 1:CH * c + CH],
                                           fours(src)[:, h, :], ALU.mult, ALU.add).then_inc(state_done, 1)
                    did(state_done)

            def gla_update01():
                v.wait_ge(state_first, 1)
                v.wait_ge(upd_full, 1)
                own.order()
                carry(1, aux23)

            def gla_update2():
                v.wait_ge(upd_full, 2)
                own.order()
                carry(2, aux01)

            def r_gate(g):
                v.wait_ge(r_silu, g + 1)
                v.wait_ge(gla_in, 48)
                own.order()
                part = gla_r[:, :, N * g:N * g + N].rearrange("p m (h e) -> p m h e", e=GDV)
                for m in range(M):
                    v.tensor_tensor(part[:, m], part[:, m], w_row[:].unsqueeze(1).to_broadcast([P, 2, GDV]),
                                    ALU.mult).then_inc(vec_step, 1)
                    did()

            def head_factors(count, width):
                own.order()
                v.tensor_scalar(ssh, ssh, 1.0 / width, EPS, ALU.mult, ALU.add).then_inc(z_sum, 1)
                did(z_sum)
                v.wait_ge(z_r, count)

            def gla_norm():
                v.wait_ge(og_sq, 8)
                head_factors(1, GDV)
                own.order()
                for m in range(M):
                    for h in range(GH):
                        s = yg_done if (m, h) == (M - 1, GH - 1) else vec_step
                        part = gla_r[:, m, GDV * h:GDV * h + GDV]
                        v.scalar_tensor_tensor(part, fours((aux23, aux01)[m])[:, h, :],
                                               rr[:, GH * m + h:GH * m + h + 1], part,
                                               ALU.mult, ALU.mult).then_inc(s, 1)
                        did(s)

            def ffn_up(b, it, part, g, value):
                dst = (f_gate, f_val)[part]
                if b == 1:
                    evac_flipped(g, dst, value)
                else:
                    if part == 0:
                        own.order()
                        v.tensor_copy(conv_now[:], conv_cols[:, :, :, bass.ds(it * KU, KU)] if not isinstance(it, int)
                                      else conv_cols[:, :, :, it * KU:it * KU + KU]).then_inc(vec_step, 1)
                        did()
                    evac_flipped(g, up_in[:, :, TAPS - 1:TAPS - 1 + T], value)
                    v.wait_ge(conv_a, it * 8 + 4 * (part + 1))
                    own.order()
                    for tap in (1, 0):
                        for f in range(KU):
                            s = vec_step if tap else conv_b
                            v.scalar_tensor_tensor(dst[:, f, :], up_in[:, f, tap:tap + T],
                                                   conv_now[:, tap, part, f:f + 1], dst[:, f, :],
                                                   ALU.mult, ALU.add).then_inc(s, 1)
                            did(s)
                        if tap:
                            own.order()
                if part == 1:
                    f = FFN[b]
                    v.wait_ge(act_f, it + (f["it0"] + 1))
                    own.order()
                    v.tensor_tensor(f_val, f_gate, f_val, ALU.mult).then_inc(f_full, 1)
                    did(f_full)
                    v.wait_ge(f_hi, it + (f["it0"] + 1))
                    own.order()
                    v.tensor_tensor(act_lo[f["f_act"]][:, 0:KU, :], f_val, act_hi[f["f_act"]][:, 0:KU, :],
                                    ALU.subtract).then_inc(f_done, 1)
                    did(f_done)

            def ffn(b):
                f = FFN[b]
                u0, g0 = f["u"], f["g"]
                for j in range(8):
                    remainder(u0 + j + SPL)
                    for name, *args in after.get(u0 + j, ()):
                        if name in tasks:
                            tasks[name](*args)
                    if j == 3:
                        ffn_up(b, 0, 0, g0, u0 + 4)
                    if j == 7:
                        ffn_up(b, 0, 1, g0 + 1, u0 + 8)
                own.order()
                with v.Fori(0, FS - 1) as i:
                    per = [(acc_free, 6), (f_full, 1), (f_done, 1)] + [(vec_step, 9), (conv_b, 8)] * (b == 0)
                    own.enter(i, per, f_done)
                    for j in range(12):
                        remainder_at(i, u0 + 8 + j + SPL)
                        if j == 3:
                            ffn_up(b, i + 1, 0, g0 + 2, i * 12 + (u0 + 12))
                        if 4 <= j < 8:
                            n = j - 4
                            v.wait_ge(unit_used, i * 12 + (u0 + 8 + j + 1))
                            own.order()
                            v.tensor_tensor(xc(n), acc[:, (g0 + 3 + n) % 2, :, :], xc(n),
                                            ALU.add).then_inc(acc_free, 1)
                            did(acc_free)
                        if j == 11:
                            ffn_up(b, i + 1, 1, g0 + 7, i * 12 + (u0 + 20))
                    own.leave(FS - 1, f_done)

            def ple_gate(g, n, b):
                if b == 0 and n:
                    v.wait_ge(squared, 24 + 4 * n)
                v.wait_ge(unit_used, full(g))
                v.wait_ge(r_done, 3 if b == 0 else 6)
                own.order()
                if b:
                    v.wait_ge(ple_tab[b], 16)
                for m in range(M):
                    s = acc_free if m == M - 1 else vec_step
                    if b == 0:
                        v.tensor_scalar(ple_t[:, m, :], acc[:, g % 2, m, :], r_col[:, m:m + 1], None,
                                        ALU.mult).then_inc(s, 1)
                    else:
                        v.scalar_tensor_tensor(ple_t[:, m, :], acc[:, g % 2, m, :], r_col[:, m:m + 1],
                                               wf_b[:, N * n:N * n + N], ALU.mult, ALU.add).then_inc(s, 1)
                    did(s)

            def ple_add(g, n, b):
                v.wait_ge(sig_done, NG * b + n + 1)
                v.wait_ge(unit_used, full(g))
                own.order()
                v.tensor_tensor(ple_t, acc[:, g % 2, :, :], ple_t, ALU.mult).then_inc(acc_free, 1)
                did(acc_free)
                own.order()
                if b:
                    v.tensor_tensor(xc(n), ple_t, xc(n), ALU.add).then_inc(x_fresh, 1)
                    did(x_fresh)
                    return
                v.tensor_tensor(ple_t, ple_t, xc(n), ALU.add).then_inc(x_fresh, 1)
                did(x_fresh)
                v.wait_ge(ple_tab[b], 16)
                own.order()
                v.tensor_tensor(xc(n), ple_t, wf_b[:, N * n:N * n + N].unsqueeze(1).to_broadcast([P, M, N]),
                                ALU.mult).then_inc(x_fresh, 1)
                did(x_fresh)

            def swapped(src, m):
                return src.rearrange("p (h s e) -> p h s e", s=2, e=HD // 2)[:, :, ::-1, :]

            def rope_tables():
                v.wait_ge(tab_in, 16 * 6)
                own.order()
                for kind in (1, 0):
                    w = w_row[:, HD * kind:HD * kind + HD]
                    other = w.rearrange("p (s e) -> p s e", s=2)[:, ::-1, :]
                    for m in range(M):
                        v.tensor_tensor(rope[kind][:, m, 0, :], rope[0][:, m, 0, :], w, ALU.mult).then_inc(vec_step, 1)
                        did()
                        v.tensor_tensor(rope[kind][:, m, 1, :].rearrange("p (s e) -> p s e", s=2),
                                        rope[0][:, m, 1, :].rearrange("p (s e) -> p s e", s=2),
                                        other, ALU.mult).then_inc(vec_step, 1)
                        did()
                    own.order()

            def rope_group(g, q, kind, h):
                if q == 0:
                    v.wait_ge(x_stored, 16 * NG)
                    rope_tables()
                if q:
                    v.wait_ge(qk_full, q)
                evac(g, z)
                own.order()
                if kind[0] == "a":
                    v.wait_ge(z_sq, (0, 1, 2, 3)[q] + 1)
                    v.tensor_reduce(ssh, z1.rearrange("p m (h e) -> p (m h) e", e=HD), AX_X, ALU.add).then_inc(vec_step, 1)
                    did()
                    head_factors(2 + q, HD)
                    own.order()
                tab = rope[2] if kind[0] == "r" else rope["qk".index(kind[1])]
                four = lambda x, m: x[:, m, :].rearrange("p (h e) -> p h e", e=HD)
                for m in range(M):
                    v.tensor_tensor(four(z1, m), four(z, m), tab[:, m, 0, :].unsqueeze(1).to_broadcast([P, 4, HD]),
                                    ALU.mult).then_inc(vec_step, 1)
                    did()
                    sine = tab[:, m, 1, :].rearrange("p (s e) -> p s e", s=2).unsqueeze(1).to_broadcast([P, 4, 2, HD // 2])
                    v.tensor_tensor(z2[:, m, :].rearrange("p (h s e) -> p h s e", s=2, e=HD // 2), swapped(z[:, m, :], m),
                                    sine, ALU.mult).then_inc(vec_step, 1)
                    did()
                own.order()
                s = vec_step if kind[0] == "a" else roped
                v.tensor_tensor(z1, z1, z2, ALU.add).then_inc(s, 1)
                did(s)
                if kind[0] == "a":
                    own.order()
                    eight = z1.rearrange("p m (h e) -> p (m h) e", e=HD)
                    v.tensor_tensor(eight, eight, rr.unsqueeze(2).to_broadcast([P, 8, HD]), ALU.mult).then_inc(roped, 1)
                    did(roped)
                if kind == "rk":
                    own.order()
                    v.tensor_tensor(k_dec[h].rearrange("p (h e) -> p h e", e=HD), four(z1, 0),
                                    k_decay[:, 4 * h:4 * h + 4].unsqueeze(2).to_broadcast([P, 4, HD]),
                                    ALU.mult).then_inc(vec_step, 1)
                    did()

            def ret_gate(h):
                v.wait_ge(r_silu, 3 + h)
                v.wait_ge(ret_tab_in, 48 * (h + 1))
                own.order()
                v.tensor_tensor(ret_g[h], ret_g[h], g_ret.unsqueeze(1).to_broadcast([P, M, N]),
                                ALU.mult).then_inc(vec_step, 1)
                did()

            def ret_scores(h):
                v.wait_ge(s_full, h + 1)
                own.order()
                v.tensor_tensor(half_k[h].rearrange("p h (m i) -> p h m i", m=M),
                                aux01.rearrange("p (h m i) -> p h m i", h=4, m=M),
                                decay_m.unsqueeze(2).to_broadcast([P, 4, M, P]), ALU.mult).then_inc(s_decayed, 1)
                did(s_decayed)
                v.tensor_tensor(half_q[h][:, :, P:T], half_q[h][:, :, P:T], q_decay, ALU.mult).then_inc(s_decayed, 1)
                did(s_decayed)

            def ret_out(h):
                v.wait_ge(og_sq, 9 + h)
                own.order()
                v.tensor_reduce(ssh, half_k[h].rearrange("p h (s e) -> p (h s) e", e=HD), AX_X,
                                ALU.add).then_inc(vec_step, 1)
                did()
                head_factors(6 + h, HD)
                own.order()
                for m in range(M):
                    for n in range(4):
                        s = yg_done if (m, n) == (M - 1, 3) else vec_step
                        part = ret_g[h][:, m, HD * n:HD * n + HD]
                        v.scalar_tensor_tensor(part, aux[:, 2 + m, HD * n:HD * n + HD], rr[:, 4 * m + n:4 * m + n + 1],
                                               part, ALU.mult, ALU.mult).then_inc(s, 1)
                        did(s)

            tasks = dict(turn=turn, norm_sums=norm_sums, norm_row=norm_row, final_sums=final_sums, evac=evac,
                         evac_flipped=evac_flipped, residual=residual, scores=scores, normalise=normalise,
                         weigh=weigh, rank_out=rank_out, rank_turn=rank_turn, gate_logits=gate_logits,
                         gate_sums=gate_sums, gla_scores=gla_scores, gla_update01=gla_update01,
                         gla_update2=gla_update2, r_gate=r_gate, gla_norm=gla_norm, ple_gate=ple_gate,
                         ple_add=ple_add, rope=rope_group, ret_gate=ret_gate, ret_scores=ret_scores,
                         ret_out=ret_out)
            v.memset(ones[:], 1.0).then_inc(vec_step, 1)
            did()
            v.memset(half_neg, -0.5).then_inc(ones_done, 1)
            did(ones_done)
            v.wait_ge(cols_full, 1)
            v.tensor_copy(vec_cols[:], aux[:, 2, 0:6 * DK]).then_inc(cols_done, 1)
            did(cols_done)
            v.tensor_copy(conv_cols[:].rearrange("p t s f -> p (t s f)"),
                          aux[:, 3, 0:8 * FT]).then_inc(cols_done, 1)
            did(cols_done)
            for u in range(SPL):
                remainder(u)
            walk(lambda u: remainder(u + SPL) if u >= 0 else None, tasks, -1, F1)
            ffn(0)
            walk(lambda u: remainder(u + SPL), tasks, PL1 - 4, F2)
            ffn(1)
            walk(lambda u: remainder(u + SPL), tasks, PL2 - 4, UNITS)

        @block.tensor
        def _(pe):
            read = {"01": [], "23": [(cols_done, 2)]}

            def free(half, *read_by):
                for s, n in read[half]:
                    pe.wait_ge(s, n)
                read[half] = list(read_by)

            def products(act_b, k, wk, slot, flipped, s, width, start, stop):
                xh, xl = act_hi[act_b], act_lo[act_b]
                wh = w_hi[:, slot, wk * width:wk * width + width]
                wl = w_lo[:, slot, wk * width:wk * width + width]
                mm = None
                if flipped:
                    flat = acc[:, s, :, :].rearrange("p b n -> p (b n)")
                    for f in range(KU):
                        c = slice(P * f, P * f + P)
                        for n, (w, x) in enumerate(((wh, xh), (wh, xl), (wl, xh))):
                            mm = pe.matmul(flat[:, T * f:T * f + T], w[:, c], x[:, k, :],
                                           start=start and n == 0 and f % 2 == 0, stop=stop and n == 2,
                                           skip_group_check=True)
                else:
                    for m in range(M):
                        c = slice(P * m, P * m + P)
                        for n, (x, w) in enumerate(((xh, wh), (xh, wl), (xl, wh))):
                            mm = pe.matmul(acc[:, s, m, 0:width], x[:, k, c], w, start=start and n == 0,
                                           stop=stop and n == 2, skip_group_check=True)
                return mm

            def multiply(u):
                d, needs = units[u]
                for s, n in needs:
                    pe.wait_ge(s, n)
                if d.first and d.group >= 2:
                    pe.wait_ge(acc_free, d.group - 1)
                pe.wait_ge(lo_done, u + 1)
                for k in range(d.nk):
                    last = k == d.nk - 1
                    mm = products(d.act, d.k0 + k, k, u % SPL, d.flipped, d.group % 2,
                                  d.width, d.first and k == 0, d.last and last)
                mm.then_inc(unit_used, 1)

            def turn(t):
                d = turns[t]
                pe.wait_ge(*d.ready)
                if t == 0:
                    pe.wait_ge(const_in, 16)
                free("01", (turned, t + 1), (turn_hi, t + 1))
                for k in range(d.tiles):
                    for m in range(M):
                        mm = pe.transpose(aux01[:, T * k + P * m:T * k + P * m + P],
                                          d.src[:, m, P * k:P * k + P], ident[:])
                mm.then_inc(turn_full, 1)

            def norm_row(k):
                r = (0, 1, None, None, 2)[k]
                pe.wait_ge(diag_done, 2 * r + 2)
                pe.wait_ge(ones_done, 1)
                free("23", (row_done, r + 1))
                pe.matmul(aux[:, 2, 0:T], ones[:], diag[:], start=True, stop=True).then_inc(row_full, 1)

            def scores(p):
                if p < 8:
                    pe.wait_ge(acc_free, 3 * (p // 4) + 2)
                else:
                    pe.wait_ge(qk_copied, 2 * ((p - 8) // 2) + 2)
                free("01", (biased, 2 * p + 2))
                for hh in range(2):
                    if p < 8:
                        rows = slice(AHD * hh, AHD * hh + AHD)
                        q, k = att_q[p // 4][rows, p % 4, :], att_k[p // 4][rows, p % 4, :]
                    else:
                        h, n = (p - 8) // 2, 2 * (p % 2) + hh
                        q, k = half_q[h][:, n, :], half_k[h][:, n, :]
                    pe.matmul(aux[:, hh, 0:P], q[:, 0:P], k[:, 0:P], start=True, stop=True)
                    mm = pe.matmul(aux[:, hh, P:P + T], q[:, P:T], k, start=True, stop=True)
                mm.then_inc(scores_full, 1)

            def probs_turn(p):
                pe.wait_ge(probs_done, 4 * p + 4)
                free("23", (pt_copied, p + 1))
                for hh in range(2):
                    for n in range(3):
                        mm = pe.transpose(aux[:, 2 + hh, P * n:P * n + P], score_of(p)[:, hh, P * n:P * n + P], ident[:])
                mm.then_inc(pt_full, 1)

            def weigh(p):
                if p < 8:
                    pe.wait_ge(acc_free, 3 * (p // 4) + 3)
                else:
                    pe.wait_ge(acc_free, G_W2 + 3 * ((p - 8) // 2) + 3)
                free("23", (o_done, p + 1), (o_hi, p + 1))
                pt = probs_of(p)
                for hh in range(2):
                    if p < 8:
                        out_ap = aux[AHD * hh:AHD * hh + AHD, 2, 0:T]
                        c = slice(P * (p % 4) + AHD * hh, P * (p % 4) + AHD * hh + AHD)
                        vals = att_v[p // 4]
                    else:
                        out_ap = aux[:, 2, T * hh:T * hh + T]
                        n = 2 * (p % 2) + hh
                        c, vals = slice(HD * n, HD * n + HD), half_v[(p - 8) // 2]
                    pe.matmul(out_ap, vals[:, 0, c], pt[:, hh, 0:T], start=True, stop=False, skip_group_check=True)
                    mm = pe.matmul(out_ap[:, P:T], vals[:, 1, c], pt[:, hh, T:T + P], start=False, stop=True,
                                   skip_group_check=True)
                mm.then_inc(o_full, 1)

            def rank_turn(g):
                pe.wait_ge(gate_done, 2)
                for m in range(M):
                    mm = pe.transpose(acc[0:RANK, g % 2, 0, T + P * m:T + P * m + P], glr[:, m, :], ident[:])
                mm.then_inc(glr_full, 1)

            def gate_logits(g):
                pe.wait_ge(glr_copied, 1)
                pe.wait_ge(small_in, 32)
                for m in range(M):
                    mm = pe.matmul(acc[:, g % 2, m, :], glr_t[0:RANK + 1, P * m:P * m + P], up_aug[0:RANK + 1, :],
                                   start=True, stop=True)
                mm.then_inc(logits_full, 1)

            def gate_sums():
                pe.wait_ge(log_a_done, 1)
                pe.wait_ge(gla_in, 48)
                free("01", (exps_done, 2), (diff_done, 1))
                for h in range(GH):
                    for m in range(M):
                        mm = pe.matmul(fours(aux01)[:, h, P * m:P * m + P], log_a[:, m, GDK * h:GDK * h + GDK],
                                       cumsum_m, start=True, stop=True, skip_group_check=True)
                mm.then_inc(b_full, 1)

            def gla_scores():
                pe.wait_ge(decayed, 3)
                free("01", (at_done, 1))
                free("23", (kend_copied, 1))
                for h in range(GH):
                    for m in range(M):
                        c = slice(P * m, P * m + P)
                        pe.matmul(fours(aux01)[:, h, c], e_neg[:, h, c], gla_q[:, h, c], start=True, stop=True,
                                  skip_group_check=True)
                        mm = pe.transpose(aux[:, 2 + m, P * h:P * h + P], gla_k[:, h, c], ident[:])
                mm.then_inc(at_full, 1)

            def update(c, dst):
                rows = slice(CH * (c % 2), CH * (c % 2) + CH)
                for h in range(GH):
                    mm = pe.matmul(fours(dst)[:, h, :], k_end_nat[rows, c // 2, GDK * h:GDK * h + GDK],
                                   gla_v[rows, c // 2, GDV * h:GDV * h + GDV], start=True, stop=True,
                                   skip_group_check=True)
                return mm

            def gla_update01():
                pe.wait_ge(kend_copied, 1)
                pe.wait_ge(acc_free, 11)
                free("01", (state_first, 1))
                free("23", (state_done, 4))
                update(0, aux01)
                update(1, aux23).then_inc(upd_full, 1)

            def gla_update2():
                free("01", (state_done, 8))
                update(2, aux01).then_inc(upd_full, 1)

            def gla_out(m):
                dst, half = ((aux23, "23"), (aux01, "01"))[m]
                if m == 0:
                    pe.wait_ge(state_done, 4)
                free(half, (og_sq, 4 * m + 4), (yg_done, 1))
                for h in range(GH):
                    e = slice(GDV * h, GDV * h + GDV)
                    o = fours(dst)[:, h, :]
                    mm = pe.matmul(o, gla_at[:, 2 * h + m, :], gla_v[:, m, e], start=True, stop=False,
                                   skip_group_check=True)
                    for c in (2 * m, 2 * m + 1):
                        if c:
                            rows = slice(CH * (c % 2), CH * (c % 2) + CH)
                            mm = pe.matmul(o[rows, :], gla_q[:, h, CH * c:CH * c + CH], states[:, c - 1, h, :],
                                           start=False, stop=True, skip_group_check=True)
                mm.then_inc(og_full, 1)

            def qk_turn(q, dst):
                pe.wait_ge(roped, q + 1)
                free("01", (qk_copied, q + 1))
                for h in range(4):
                    for m in range(M):
                        mm = pe.transpose(fours(aux01)[:, h, P * m:P * m + P], z1[:, m, HD * h:HD * h + HD], ident[:])
                mm.then_inc(qk_full, 1)

            def ret_scores(h):
                pe.wait_ge(qk_copied, 6 + 2 * h)
                pe.wait_ge(acc_free, G_W2 + 9 + 4 * h)
                free("01", (s_decayed, 2 * h + 2))
                free("23", (s_state, h + 1))
                for n in range(4):
                    for m in range(M):
                        c = slice(P * m, P * m + P)
                        pe.matmul(fours(aux01)[:, n, c], half_k[h][:, n, c], half_q[h][:, n, c], start=True,
                                  stop=True, skip_group_check=True)
                    c = slice(HD * n, HD * n + HD)
                    mm = pe.matmul(aux[:, 2, c], k_dec[h][:, c], ret_v[h][:, 0, c], start=True, stop=True,
                                   skip_group_check=True)
                mm.then_inc(s_full, 1)

            def ret_out(h):
                pe.wait_ge(s_decayed, 2 * h + 2)
                free("23", (og_sq, 9 + h), (yg_done, 2 + h))
                for n in range(4):
                    c = slice(HD * n, HD * n + HD)
                    pe.matmul(aux[:, 2, c], half_k[h][:, n, 0:P], ret_v[h][:, 0, c], start=True, stop=True,
                              skip_group_check=True)
                    pe.matmul(aux[:, 3, c], half_k[h][:, n, P:T], ret_v[h][:, 1, c], start=True, stop=False,
                              skip_group_check=True)
                    mm = pe.matmul(aux[:, 3, c], half_q[h][:, n, P:T], k_dec[h][:, c], start=False, stop=True,
                                   skip_group_check=True)
                mm.then_inc(ret_full, 1)

            def ffn(b):
                f = FFN[b]
                u0, g0 = f["u"], f["g"]
                turn0 = (6, 21)[b]

                def part(act_b, k0, u, g, flipped, first, last):
                    for k in range(KU):
                        mm = products(act_b, k0 + k, k, u % SPL, flipped, g % 2, N, first and k == 0,
                                      last and k == KU - 1)
                    return mm

                for j in range(8):
                    q, g = j % 4, g0 + j // 4
                    if j < 4:
                        pe.wait_ge(turned, turn0 + q + 1)
                    if q == 0:
                        pe.wait_ge(acc_free, g - 1)
                    pe.wait_ge(lo_done, u0 + j + 1)
                    mm = part(f["act"], KU * q, u0 + j, g, True, q == 0, q == 3)
                    mm.then_inc(unit_used, 1)
                    for name, *args in after.get(u0 + j, ()):
                        if name in tasks:
                            tasks[name](*args)
                with pe.Fori(0, FS - 1) as i:
                    for j in range(12):
                        u, q = u0 + 8 + j, j % 4
                        down = 4 <= j < 8
                        g = g0 + 2 + (0 if j < 4 else 1 + q if down else 5)
                        if down and q == 0:
                            pe.wait_ge(f_done, i + (f["it0"] + 1))
                        if down or q == 0:
                            pe.wait_ge(acc_free, i * 6 + (g - 1))
                        pe.wait_ge(lo_done, i * 12 + (u + 1))
                        if down:
                            mm = part(f["f_act"], 0, u, g, False, True, True)
                        else:
                            mm = part(f["act"], KU * q, u, g, True, q == 0, q == 3)
                        mm.then_inc(unit_used, 1)
                for n in range(NG):
                    u, g = u0 + 12 * FS - 4 + n, (GD1, GD2)[b] + n
                    if n == 0:
                        pe.wait_ge(f_done, f["it0"] + FS)
                    pe.wait_ge(acc_free, g - 1)
                    pe.wait_ge(lo_done, u + 1)
                    part(f["f_act"], 0, u, g, False, True, True).then_inc(unit_used, 1)
                    for name, *args in after.get(u, ()):
                        if name in tasks:
                            tasks[name](*args)

            tasks = dict(turn=turn, norm_row=norm_row, scores=scores, probs_turn=probs_turn, weigh=weigh,
                         rank_turn=rank_turn, gate_logits=gate_logits, gate_sums=gate_sums, gla_scores=gla_scores,
                         gla_update01=gla_update01, gla_update2=gla_update2, gla_out0=lambda: gla_out(0),
                         gla_out1=lambda: gla_out(1), qk_turn=qk_turn, ret_scores=ret_scores, ret_out=ret_out)
            pe.wait_ge(const_in, 16)
            pe.wait_ge(vec_in, 16 * (len(VEC_ROWS) + 2))
            n = DK * len(VEC_ROWS)
            pe.transpose(aux[:, 2, 0:n], vec_rows[0:n, :], ident[0:n, 0:n])
            for t in range(TAPS + 1):
                mm = pe.transpose(aux[:, 3, 2 * FT * t:2 * FT * t + 2 * FT], conv_rows[0:2 * FT, t, :],
                                  ident[0:2 * FT, 0:2 * FT])
            mm.then_inc(cols_full, 1)
            walk(lambda u: multiply(u) if u >= 0 else None, tasks, -1, F1)
            ffn(0)
            walk(multiply, tasks, PL1, F2)
            ffn(1)
            walk(multiply, tasks, PL2, UNITS)

        @block.gpsimd
        def _(pool):
            def rsqrt(dst, src, width, done):
                pool.tensor_tensor(dst, src, half_neg[:, 0:width], ALU.pow).then_inc(done, 1)

            def norm_factor(mean_count):
                pool.wait_ge(mean_done, mean_count)
                rsqrt(r_col, mean1, M, r_done)

            def head_factor(count):
                pool.wait_ge(z_sum, count)
                rsqrt(rr, ssh, 8, z_r)

            pool.dma_start(cumsum_m, a["c_cumsum"]).then_inc(gla_in, 16)
            pool.dma_start(chunk_mask.bitcast(U32), a["c_chunk_mask"]).then_inc(gla_in, 16)
            pool.dma_start(w_row[:], a["gla_norm_w"][0].partition_broadcast(P)).then_inc(gla_in, 16)
            pool.wait_ge(ones_done, 1)
            norm_factor(1)
            pool.dma_start(up_aug[0:RANK, :], a["w_gla_gate_up"][0]).then_inc(small_in, 16)
            pool.dma_start(up_aug[RANK:RANK + 1, :], a["b_gla_gate"]).then_inc(small_in, 16)
            rel = a["att_rel_bias"]
            for p in range(8):
                if p >= 2:
                    pool.wait_ge(biased, 2 * (p - 2) + 2)
                src = bass.AP(tensor=rel.tensor, offset=2 * p * (2 * REL + 1) + REL - P + 1,
                              ap=[[1, P], [2 * REL + 1, 2], [1, T]])
                pool.dma_start(bias[p % 2], src).then_inc(bias_in[p % 2], 16)
            head_factor(1)
            pool.wait_ge(turn_full, 6)
            pool.dma_start(x_sb, x_dram).then_inc(x_back, 16)
            pool.dma_start(p_sb, a["p"][0, 0].rearrange("(m p) n -> p m n", p=P)).then_inc(ple_in[0], 16)
            pool.dma_start(wf_b, a["final_norm_w"].partition_broadcast(P)).then_inc(ple_tab[0], 16)
            norm_factor(2)
            norm_factor(3)
            pool.wait_ge(x_fresh, 1)
            pool.dma_start(rope[0], a["c_rope_a"]).then_inc(tab_in, 16)
            pool.dma_start(rope[2], a["c_rope_r"]).then_inc(tab_in, 16)
            pool.dma_start(w_row[:, 0:HD], a["q_norm_2"][0].partition_broadcast(P)).then_inc(tab_in, 16)
            pool.dma_start(w_row[:, HD:2 * HD], a["k_norm_2"][0].partition_broadcast(P)).then_inc(tab_in, 16)
            pool.dma_start(k_decay, a["c_k_decay"]).then_inc(tab_in, 16)
            pool.dma_start(causal[:], a["c_causal"]).then_inc(tab_in, 16)
            for n in range(NG):
                pool.wait_ge(x_fresh, 2 * n + 2)
                pool.dma_start(spill[:, :, N * n:N * n + N], xc(n)).then_inc(x_stored, 16)
            pool.wait_ge(mean_done, 4)
            rsqrt(r_final, mean1, M, pool_step)
            pool.wait_ge(mean_done, 5)
            rsqrt(r_col, mean2, M, r_done)
            for q in range(4):
                head_factor(2 + q)

            def ret_tables(h):
                pool.dma_start(decay_m, a["c_decay"][:, 4 * h:4 * h + 4, :]).then_inc(ret_tab_in, 16)
                pool.dma_start(q_decay.rearrange("p a b -> p (a b)"),
                               a["c_q_decay"][0, N * h:N * h + N].partition_broadcast(P)).then_inc(ret_tab_in, 16)
                pool.dma_start(g_ret, a["g_ret_2"][0, N * h:N * h + N].partition_broadcast(P)).then_inc(ret_tab_in, 16)

            pool.wait_ge(o_done, 12)
            ret_tables(0)
            head_factor(6)
            pool.wait_ge(yg_done, 2)
            ret_tables(1)
            head_factor(7)
            pool.wait_ge(turn_full, 21)
            pool.wait_ge(x_stored, 16 * NG)
            pool.dma_start(x_sb, spill).then_inc(x_back, 16)
            pool.dma_start(p_sb, a["p_2"][0, 0].rearrange("(m p) n -> p m n", p=P)).then_inc(ple_in[1], 16)
            pool.dma_start(wf_b, a["b_ple_gate_2"][0].partition_broadcast(P)).then_inc(ple_tab[1], 16)
            norm_factor(6)
            norm_factor(7)
            for n in range(NG):
                pool.wait_ge(x_fresh, 2 * NG + n + 1)
                pool.dma_start(out_dram[:, :, N * n:N * n + N], xc(n)).then_inc(out_stored, 16)


_INS = ["x", "p", "norm_mix_w", "w_in", "att_rel_bias", "w_gla_gate_up", "b_gla_gate", "gla_norm_w", "w_out",
        "norm_ffn_w", "w_ffn_up", "w_ffn_conv", "b_ffn_conv", "w_ffn_down", "norm_ple_w", "w_ple_gate",
        "w_ple_proj", "final_norm_w", "p_2", "g_mix_2", "w_in_2", "q_norm_2", "k_norm_2", "g_ret_2", "w_o_2",
        "g_ffn_2", "w_gate_2", "w_up_2", "w_down_2", "g_ple_2", "w_ple_gate_2", "b_ple_gate_2", "w_ple_proj_2"]


def kernel(**inputs):
    import concourse.bacc as _bacc
    from concourse.bass_utils import run_bass_kernel_spmd as _run

    nc = _bacc.Bacc("TRN2", target_bir_lowering=False, num_devices=1)
    arrays, views = {}, {}
    for name in _INS:
        arr = np.ascontiguousarray(inputs[name])
        arrays[f"in_{name}"] = arr
        views[name] = nc.dram_tensor(f"in_{name}", arr.shape, mybir.dt.from_np(arr.dtype), kind="ExternalInput").ap()
    for name, arr in shape_constants().items():
        arrays[name] = arr
        views[name] = nc.dram_tensor(name, arr.shape, mybir.dt.from_np(arr.dtype), kind="ExternalInput").ap()
    out = nc.dram_tensor("out", (1, T, D), F32, kind="ExternalOutput").ap()
    x_spill = nc.dram_tensor("x_spill", (T, D), F32, kind="Internal").ap()
    build_two_blocks(nc, views, out, x_spill)
    r = _run(nc, [arrays], core_ids=[0])
    return r.results[0]["out"]
```

```python
from contextlib import ExitStack
from typing import NamedTuple

import numpy as np

import concourse.bass as bass
from concourse import mybir

F32 = mybir.dt.float32
F32R = mybir.dt.float32r
U32 = mybir.dt.uint32
ALU = mybir.AluOpType
ACT = mybir.ActivationFunctionType
AX_X = mybir.AxisListType.X

P = 128
T = 256
M = T // P
D = 2048
DK = D // P
N = 512
NG = D // N
KU = 4
FF = 5632
FT = FF // P
FS = FF // N
PLE = 256
EPS = 1e-6
NEG = -1e30

CH = 64
AHD = 64
REL = 256
GH, GDK, GDV, RANK = 4, 128, 256, 16
AW = GW = D // 2
GKW = GW // 2
TAU = 16.0
HD, H2 = 128, 8

RAW = 4
SPL = 3
TAPS = 3

VEC_ROWS = ["norm_mix_w", "norm_ffn_w", "norm_ple_w", "g_mix_2", "g_ffn_2", "g_ple_2"]


class Unit(NamedTuple):
    src: object
    nk: int
    width: int
    flipped: bool
    act: int
    k0: int
    group: int
    first: bool
    last: bool


class Turn(NamedTuple):
    src: object
    tiles: int
    act: int
    k0: int
    col: object
    ready: tuple
    half: str = "01"


class Own:

    def __init__(self, eng):
        self.eng, self.n, self.last, self.i, self.per = eng, {}, None, None, {}

    def did(self, sem):
        base = self.n[sem.num] = self.n.get(sem.num, 0) + 1
        self.last = (sem, base if self.i is None else self.i * self.per[sem.num] + base)

    def order(self):
        self.eng.wait_ge(*self.last)

    def enter(self, i, per, last):
        self.i, self.per, self.start = i, {s.num: v for s, v in per}, dict(self.n)
        self.last = (last, i * self.per[last.num] + self.n[last.num])

    def leave(self, rounds, last):
        for num, v in self.per.items():
            assert self.n[num] - self.start.get(num, 0) == v, (num, self.n[num], self.start.get(num), v)
            self.n[num] = self.start.get(num, 0) + v * rounds
        self.i = None
        self.last = (last, self.n[last.num])


def shape_constants():
    c = {}
    c["c_ident"] = np.eye(P, dtype=np.float32)
    j, i = np.meshgrid(np.arange(P), np.arange(P), indexing="ij")
    same = (j // CH == i // CH) & (j <= i)
    c["c_cumsum"] = (same / TAU).astype(np.float32)
    c["c_chunk_mask"] = same.astype(np.uint32)
    causal = np.zeros((P, T), np.float32)
    causal[:, P:] = np.where(i <= j, 0.0, NEG)
    c["c_causal"] = causal
    pos = np.arange(T, dtype=np.float32)[:, None]
    half = HD // 2
    for name, freq in (
        ("c_rope_a", np.power(np.float32(10000.0), -np.arange(0, HD, 2, dtype=np.float32) / np.float32(HD))),
        ("c_rope_r", np.power(np.float32(10000.0), -np.linspace(0.0, 1.0, half, dtype=np.float32))),
    ):
        ang = pos * freq[None, :].astype(np.float32)
        cos, sin = np.cos(ang).astype(np.float32), np.sin(ang).astype(np.float32)
        both = np.stack([np.concatenate([cos, cos], 1), np.concatenate([-sin, sin], 1)], 1)
        c[name] = np.ascontiguousarray(both.reshape(M, P, 2, HD).transpose(1, 0, 2, 3))
    log_g = np.log(1.0 - np.power(2.0, -5.0 - np.arange(H2)))
    rel = (i - j)[:, None, :]
    decay = np.where(rel >= 0, np.exp(log_g[None, :, None] * np.maximum(rel, 0)), 0.0)
    c["c_decay"] = (decay * HD ** -0.5).astype(np.float32)
    c["c_q_decay"] = np.exp(log_g[:, None] * (np.arange(P)[None, :] + 1.0)).astype(np.float32).reshape(1, H2 * P)
    c["c_k_decay"] = (np.exp(log_g[None, :] * (P - 1.0 - np.arange(P)[:, None])) * HD ** -0.5).astype(np.float32)
    return c


def build_two_blocks(nc, a, out, x_spill):
    ctx = ExitStack()
    with ctx:
        def sb(name, shape, dt=F32):
            return ctx.enter_context(nc.sbuf_tensor(name, shape, dt))

        def sem(name):
            return ctx.enter_context(nc.semaphore(name))

        w_lo = sb("w_lo", [P, SPL, KU * N], F32R)
        raw = sb("raw", [P, RAW, KU * N])
        w_hi = sb("w_hi", [P, SPL, KU * N], F32R)
        act_hi = [sb(f"act_hi{b}", [P, DK, T], F32R) for b in range(2)]
        act_lo = [sb(f"act_lo{b}", [P, DK, T], F32R) for b in range(2)]
        SC = 14336
        mem = sb("mem", [P, SC])
        ident = sb("ident", [P, P])
        ones = sb("ones", [P, P])
        diag = sb("diag", [P, T])
        r_row = sb("r_row", [P, T])
        vec_cols = sb("vec_cols", [P, 6 * DK])
        conv_cols = sb("conv_cols", [P, TAPS + 1, 2, FT])
        conv_now = sb("conv_now", [P, TAPS + 1, 2, KU])
        stat = sb("stat", [P, 256])

        x_sb = mem[:, 0:M * D].rearrange("p (m n) -> p m n", m=M)

        def view(at, *dims):
            n = int(np.prod(dims))
            assert at + n <= SC
            v = mem[:, at:at + n]
            if len(dims) == 2:
                return v.rearrange("p (a b) -> p a b", a=dims[0])
            if len(dims) == 3:
                return v.rearrange("p (a b c) -> p a b c", a=dims[0], b=dims[1])
            return v

        ssq1 = stat[:, 0:8].rearrange("p (n m) -> p n m", m=M)
        ssq2 = stat[:, 8:16].rearrange("p (n m) -> p n m", m=M)
        mean1, mean2 = stat[:, 16:18], stat[:, 18:20]
        r_col = stat[:, 20:22]
        r_final = stat[:, 22:24]
        half_neg = stat[:, 24:40]
        mx = stat[:, 40:44].rearrange("p (t h) -> p t h", t=M)
        den = stat[:, 44:48].rearrange("p (t h) -> p t h", t=M)
        rden = stat[:, 48:52].rearrange("p (t h) -> p t h", t=M)
        ssh = stat[:, 52:60]
        rr = stat[:, 60:68]
        k_decay = stat[:, 100:108]
        decay_cols = stat[:, 112:128]

        acc = ctx.enter_context(nc.psum_tensor("acc", [P, 2, M, N], F32))
        aux = ctx.enter_context(nc.psum_tensor("aux", [P, 4, N], F32))
        aux01 = aux[:, 0:2, :].rearrange("p b n -> p (b n)")
        aux23 = aux[:, 2:4, :].rearrange("p b n -> p (b n)")
        half_of = {"01": aux01, "23": aux23}

        att_q = [view(3072 * h, 4, T) for h in range(2)]
        att_k = [view(3072 * h + 1024, 4, T) for h in range(2)]
        att_v = [view(3072 * h + 2048, M, N) for h in range(2)]
        BIAS = 6144
        bias = [view(BIAS + 512 * b, 2, T) for b in range(2)]
        scores_sb = view(7168, 2, 384)
        probs_t = view(8192, 2, 384)
        gla_q, gla_k = view(9216, GH, T), view(10240, GH, T)
        log_a = view(11264, M, GKW)
        k_end_nat = view(11264, M, GKW)
        e_diff = view(11264, GH, T)
        e_pos, e_neg = view(12288, GH, T), view(13312, GH, T)
        cumsum_m = view(7936, P)
        chunk_mask = view(8960, P)
        up_aug, glr_t = view(10240, GKW), view(10752, T)
        gla_v = view(0, M, GW)
        gla_r = view(3072, M, GW)
        gla_at = view(5120, 2 * GH, P)
        states = view(6144, 3, GH, GDV)
        neg_part = view(12288, M, GKW)
        neg_abs = view(13312, M, GKW)
        up_in = view(4096, KU, T + 2)
        f_gate = view(5248, KU, T)
        f_val = view(6272, KU, T)
        ple_t = view(4096, M, N)
        p_sb = view(7424, M, PLE)
        wf_b = view(8192, D)
        sq_junk = view(10240, N)
        vec_rows = view(4096, P)
        conv_rows = view(4224, TAPS + 1, P)

        raw_in = [sem(f"raw_in{s}") for s in range(RAW)]
        hi_done, lo_done, unit_used = sem("hi_done"), sem("lo_done"), sem("unit_used")
        acc_free = sem("acc_free")
        const_in, small_in = sem("const_in"), sem("small_in")
        x_in = [sem(f"x_in{n}") for n in range(NG)]
        mix_in, vec_in, bias_in = sem("mix_in"), sem("vec_in"), [sem("bias_in0"), sem("bias_in1")]
        cols_full, cols_done = sem("cols_full"), sem("cols_done")
        turn_full, turn_hi, turned = sem("turn_full"), sem("turn_hi"), sem("turned")
        squared = sem("squared")
        vec_step, act_step, pool_step = sem("vec_step"), sem("act_step"), sem("pool_step")
        mean_done, r_done, diag_done, row_full, row_done = (
            sem("mean_done"), sem("r_done"), sem("diag_done"), sem("row_full"), sem("row_done"))
        scores_full, biased, max_done, exp_done, probs_done = (
            sem("scores_full"), sem("biased"), sem("max_done"), sem("exp_done"), sem("probs_done"))
        pt_full, pt_copied, o_full, o_hi, o_done = (
            sem("pt_full"), sem("pt_copied"), sem("o_full"), sem("o_hi"), sem("o_done"))
        state_first, ones_done, gla_in = sem("state_first"), sem("ones_done"), sem("gla_in")
        ple_tab = [sem("ple_tab0"), sem("ple_tab1")]
        conv_a, conv_b, act_f, f_full, f_hi, f_done = (
            sem("conv_a"), sem("conv_b"), sem("act_f"), sem("f_full"), sem("f_hi"), sem("f_done"))
        glr_copied, logits_full, log_a_done = sem("glr_copied"), sem("logits_full"), sem("log_a_done")
        neg_abs_done, log_done = sem("neg_abs_done"), sem("log_done")
        b_full, exps_done, diff_done, ediff_done, decayed = (
            sem("b_full"), sem("exps_done"), sem("diff_done"), sem("ediff_done"), sem("decayed"))
        at_full, at_done, kend_copied, upd_full, state_done = (
            sem("at_full"), sem("at_done"), sem("kend_copied"), sem("upd_full"), sem("state_done"))
        og_full, og_sq, og_r, r_silu, yg_done = (
            sem("og_full"), sem("og_sq"), sem("og_r"), sem("r_silu"), sem("yg_done"))
        ple_in, sig_done, x_fresh, x_stored, x_back = (
            [sem("ple_in0"), sem("ple_in1")], sem("sig_done"), sem("x_fresh"), sem("x_stored"), sem("x_back"))
        z_done, z_sq, z_sum, z_r, roped, qk_full, qk_copied = (
            sem("z_done"), sem("z_sq"), sem("z_sum"), sem("z_r"), sem("roped"), sem("qk_full"), sem("qk_copied"))
        s_full, s_decayed, u_full, s_state, ret_full = (
            sem("s_full"), sem("s_decayed"), sem("u_full"), sem("s_state"), sem("ret_full"))
        tab_in, ret_tab_in, out_stored = sem("tab_in"), sem("ret_tab_in"), sem("out_stored")

        BASE2 = 10752
        half_q = [view(3072 * h, 4, T) for h in range(2)]
        half_k = [view(3072 * h + 1024, 4, T) for h in range(2)]
        half_v = [view(3072 * h + 2048, M, N) for h in range(2)]
        k_dec = [view(3072 * h + 2048, N) for h in range(2)]
        ret_v = [view(12288, M, N), view(7680, M, N)]
        ret_g = [view(13312, M, N), view(8704, M, N)]
        z, z1, z2 = view(7680, M, N), view(8704, M, N), view(9728, M, N)
        decay_m, q_decay = view(6144, 4, P), view(6656, 4, P)
        g_ret = view(7168, N)
        rope = [view(BASE2 + 512 * n, M, 2, HD) for n in range(3)]
        causal = diag
        score_of = lambda p: scores_sb if p < 8 else view(6144, 2, 384)
        probs_of = lambda p: probs_t if p < 8 else view(6912, 2, 384)
        w_row = sb("w_row", [P, 2 * HD])

        def rows(ap):
            return ap.rearrange("(k p) n -> p k n", p=P)

        w_in1, w_out1 = rows(a["w_in"][0]), rows(a["w_out"][0])
        w_up1, w_down1 = rows(a["w_ffn_up"][0]), rows(a["w_ffn_down"][0])
        w_pg1, w_pp1 = rows(a["w_ple_gate"][0]), rows(a["w_ple_proj"][0])
        w_in2, w_out2 = rows(a["w_in_2"][0]), rows(a["w_o_2"][0])
        w_gate2, w_up2, w_down2 = rows(a["w_gate_2"][0]), rows(a["w_up_2"][0]), rows(a["w_down_2"][0])
        w_pg2, w_pp2 = rows(a["w_ple_gate_2"][0]), rows(a["w_ple_proj_2"][0])
        x_dram = a["x"][0].rearrange("(m p) n -> p m n", p=P)
        out_dram = out[0].rearrange("(m p) n -> p m n", p=P)
        spill = x_spill.rearrange("(m p) n -> p m n", p=P)

        units, after = [], {}

        def unit(w, col, width, flipped, act, k0, nk, group, first, last, needs=()):
            src = w[:, k0:k0 + nk, col:col + width]
            units.append((Unit(src, nk, width, flipped, act, k0, group, first, last), needs))

        def whole(w, col, flipped, act, group, needs):
            for q in range(4):
                unit(w, col, N, flipped, act, KU * q, KU, group, q == 0, q == 3, needs(q))

        def then(slot, *task):
            after.setdefault(slot, []).append(task)

        for n in range(NG):
            then(-4 + n // 2, "turn", n)
            then(-1 + n // 2, "square_first", n)
        then(1, "norm_sums", 0)
        then(2, "norm_diag", 0)
        then(3, "norm_row", 0)
        then(4, "tables")
        xt0 = lambda q: [(turned, q + 1)]
        qc, kc, vc = 0, AW, 2 * AW
        for h in range(2):
            for n, (col, flipped) in enumerate(((qc, True), (kc, True), (vc, False))):
                g = 3 * h + n
                whole(w_in1, col + N * h, flipped, 0, g, xt0)
                dst = (att_q, att_k, att_v)[n][h]
                then(4 * g + 3, "evac_flipped" if flipped else "evac", g, dst)
        unit(w_in1, 3 * AW + 2 * GKW + 2 * GW, RANK, True, 0, 0, DK, 6, True, True)
        then(24, "rank_out", 6)
        then(26, "gate_logits", 6)
        then(27, "gate_logs")
        gc = 3 * AW
        g1 = [(gc, True, gla_q), (gc + GKW, True, gla_k), (gc + 2 * GKW, False, gla_v[:, :, 0:N]),
              (gc + 2 * GKW + N, False, gla_v[:, :, N:2 * N]), (gc + 2 * GKW + GW, False, gla_r[:, :, 0:N]),
              (gc + 2 * GKW + GW + N, False, gla_r[:, :, N:2 * N])]
        for n, (col, flipped, dst) in enumerate(g1):
            whole(w_in1, col, flipped, 0, 7 + n, xt0)
            then(28 + 4 * n, "evac_flipped" if flipped else "evac", 7 + n, dst)
        then(44, "r_gate", 0)
        then(48, "r_gate", 1)
        for h in range(2):
            for j in range(4):
                at = 12 + 12 * h + 3 * j
                p = 4 * h + j
                then(at, "scores", p)
                then(at + 1, "normalise", p)
                then(at + 2, "probs_turn", p)
                then(at + 3, "weigh", p)
        for slot, task in ((37, "gate_sums"), (38, "decay"), (39, "gla_scores"), (41, "gla_update01"),
                           (43, "gla_update2"),
                           (44, "gla_out0"), (46, "gla_out1"), (48, "gla_norm")):
            then(slot, task)
        ORDER = {"norm_row": -1, "evac": 0, "evac_flipped": 0, "weigh": 1, "probs_turn": 2, "scores": 3, "normalise": 3}
        for slot in after:
            after[slot].sort(key=lambda task: ORDER.get(task[0], 4))

        u = len(units)
        W1 = u
        assert u == 49
        yt0 = lambda q: [(o_done, 4), (o_done, 8), (turned, 5), (turned, 6)][q:q + 1]
        for n, qs in ((0, (0, 1)), (1, (0, 1)), (0, (2, 3)), (1, (2, 3)), (2, range(4)), (3, range(4))):
            for q in qs:
                unit(w_out1, N * n, N, False, 1, KU * q, KU, 13 + n, q == 0, q == 3, yt0(q))
        then(u + 2, "turn", 4)
        then(u + 3, "turn", 5)
        for n, at in enumerate((5, 7, 11, 15)):
            then(u + at, "residual", 13 + n, n, 0)
            then(u + at, "square_x", 13 + n, n)
            then(u + at + 2, "turn", 6 + n)
        then(u + 16, "norm_sums", 1)
        then(u + 17, "norm_diag", 1)
        then(u + 18, "norm_row", 1)
        F1 = len(units)
        units += [None] * (12 * FS)
        G_F1 = 17
        E1 = len(units) - 4
        GD1 = G_F1 + 2 + 6 * (FS - 1)
        for n in range(NG):
            then(E1 + n, "residual", GD1 + n, n, 1)
            then(E1 + n, "square_x", GD1 + n, n)
            then(E1 + n + 2, "turn", 11 + n)
        then(E1 + 1, "turn", 10)
        then(E1 + 4, "norm_sums", 2)

        def embedding(w_gate, w_proj, group, act, p_act, p_k0, turn0, p_turn, block):
            u = len(units)
            for n in range(NG):
                g = group + 2 * n
                whole(w_gate, N * n, False, act, g, lambda q: [(turned, turn0 + q + 1)])
                units.append((Unit(w_proj[:, :, N * n:N * n + N], 2, N, False, p_act, p_k0, g + 1, True, True),
                              [(turned, p_turn + 1)]))
                then(u + 5 * n + 3, "ple_gate", g, n, block)
                then(u + 5 * n + 4, "ple_add", g + 1, n, block)
                if block == 0:
                    then(u + 5 * n + 6, "turn", 15 + n)

        PL1 = len(units)
        G_P1 = GD1 + 4
        embedding(w_pg1, w_pp1, G_P1, 0, 1, DK - 2, 11, 10, 0)
        W2 = len(units)
        then(W2, "final_sums")
        G_W2 = G_P1 + 8
        xt1 = lambda q: [(turned, 15 + q + 1)]
        order = ["aq0", "ak0", "av0", "aq1", "ak1", "av1", "rq0", "rk0", "rv0", "rg0", "rq1", "rk1", "rv1", "rg1"]
        cols = {n: i * 2 * N for i, n in enumerate(("aq", "ak", "av", "rq", "rk", "rv", "rg"))}
        qk = 0
        for i, name in enumerate(order):
            kind, h, g, s = name[:2], int(name[2]), G_W2 + i, W2 + 4 * i + 3
            whole(w_in2, cols[kind] + N * h, False, 1, g, xt1)
            if kind in ("aq", "ak", "rq", "rk"):
                dst = (half_q if kind[1] == "q" else half_k)[h]
                then(s, "rope_in", g, qk)
                then(s, "rope", g, qk, kind, h)
                then(s + 3, "qk_turn", qk, dst)
                qk += 1
            elif kind == "rg":
                then(s, "evac", g, ret_g[h])
                then(s, "ret_gate", h)
            else:
                then(s, "evac", g, (half_v if kind == "av" else ret_v)[h])
        for p in range(8, 12):
            at = W2 + 12 + 12 * ((p - 8) // 2) + 4 * ((p - 8) % 2)
            then(at, "scores", p)
            then(at + 1, "normalise", p)
            then(at + 3, "probs_turn", p)
            then(at + 4, "weigh", p)
        for h, at in ((0, 40), (1, 56)):
            then(W2 + at, "ret_scores", h)
            then(W2 + at + 1 + (h == 0), "ret_out", h)
            then(W2 + at + 3 + (h == 0), "turn", 19 + h)
        WO2 = len(units)
        G_O2 = G_W2 + 14
        yt1 = lambda q: [(o_done, 10), (o_done, 12), (turned, 20), (turned, 21)][q:q + 1]
        for n, qs in ((0, range(3)), (1, range(3)), (0, (3,)), (1, (3,)), (2, range(4)), (3, range(4))):
            for q in qs:
                unit(w_out2, N * n, N, False, 0, KU * q, KU, G_O2 + n, q == 0, q == 3, yt1(q))
        for n, at in enumerate((6, 7, 11, 15)):
            then(WO2 + at, "residual", G_O2 + n, n, 2)
            then(WO2 + at, "square_x", G_O2 + n, n)
            then(WO2 + at + 2, "turn", 21 + n)
        then(WO2 + 16, "norm_sums", 4)
        then(WO2 + 17, "norm_diag", 2)
        then(WO2 + 18, "norm_row", 2)
        F2 = len(units)
        units += [None] * (12 * FS)
        G_F2 = G_O2 + 4
        E2 = len(units) - 4
        GD2 = G_F2 + 2 + 6 * (FS - 1)
        for n in range(NG):
            then(E2 + n, "residual", GD2 + n, n, 1)
            then(E2 + n, "square_x", GD2 + n, n)
            then(E2 + n + 2, "turn", 26 + n)
        then(E2 + 1, "turn", 25)
        then(E2 + 4, "norm_sums", 5)
        PL2 = len(units)
        G_P2 = GD2 + 4
        embedding(w_pg2, w_pp2, G_P2, 1, 0, DK - 2, 26, 25, 1)
        UNITS = len(units)

        col_of = lambda name, n: vec_cols[:, DK * VEC_ROWS.index(name) + 4 * n:DK * VEC_ROWS.index(name) + 4 * n + 4]
        xc = lambda n: x_sb[:, :, N * n:N * n + N]
        turns = [Turn(xc(n), 4, 0, 4 * n, col_of("norm_mix_w", n), (x_in[n], 16), ("01", "23")[n % 2])
                 for n in range(4)]
        turns += [Turn(gla_r[:, :, N * n:N * n + N], 4, 1, 8 + 4 * n, None, (yg_done, 1)) for n in range(2)]
        turns += [Turn(xc(n), 4, 0, 4 * n, col_of("norm_ffn_w", n), (acc_free, 14 + n)) for n in range(4)]
        turns += [Turn(p_sb, 2, 1, DK - 2, None, (ple_in[0], 16))]
        turns += [Turn(xc(n), 4, 0, 4 * n, col_of("norm_ple_w", n), (acc_free, GD1 + 1 + n)) for n in range(4)]
        turns += [Turn(xc(n), 4, 1, 4 * n, col_of("g_mix_2", n), (x_fresh, 2 * n + 2)) for n in range(4)]
        turns += [Turn(ret_g[h], 4, 0, 8 + 4 * h, None, (yg_done, 2 + h)) for h in range(2)]
        turns += [Turn(xc(n), 4, 1, 4 * n, col_of("g_ffn_2", n), (acc_free, G_O2 + 1 + n)) for n in range(4)]
        turns += [Turn(p_sb, 2, 0, DK - 2, None, (ple_in[1], 16))]
        turns += [Turn(xc(n), 4, 1, 4 * n, col_of("g_ple_2", n), (acc_free, GD2 + 1 + n)) for n in range(4)]

        def fours(v):
            return v.rearrange("p (f t) -> p f t", f=KU)

        four = range(4)
        ROUNDS = FS - 2
        FFN_HEAD = [(kind, q, 0) for kind in ("gate", "value") for q in four]
        FFN_ROUND = [("gate", q, 1) for q in four] + [("down", q, 0) for q in four] + [("value", q, 1) for q in four]
        FFN_TAIL = [(kind, q, step) for kind, step in (("gate", FS - 1), ("value", FS - 1), ("down", FS - 2),
                                                       ("down", FS - 1)) for q in four]
        FT_TAIL = len(FFN_HEAD) + ROUNDS * len(FFN_ROUND)
        G_TAIL = 2 + 6 * ROUNDS
        assert FT_TAIL + len(FFN_TAIL) == 12 * FS
        FFN = [
            dict(u=F1, g=G_F1, act=0, f_act=1, it0=0, gate=(w_up1, 0), value=(w_up1, FF), down=w_down1),
            dict(u=F2, g=G_F2, act=1, f_act=0, it0=FS, gate=(w_gate2, 0), value=(w_up2, 0), down=w_down2),
        ]

        def ffn_src(b, kind, q, step):
            at = (lambda size, base: slice(size * step + base, size * step + base + size)) if isinstance(step, int) \
                else (lambda size, base: bass.ds(step * size + base, size))
            if kind == "down":
                return FFN[b]["down"][:, at(KU, 0), N * q:N * q + N]
            w, c = FFN[b][kind]
            return w[:, KU * q:KU * q + KU, at(N, c)]

        def raw_slot(s, nk, width):
            return raw[:, s, 0:nk * width].rearrange("p (k n) -> p k n", k=nk)

        def columns(u):
            return units[u][0].nk * units[u][0].width if units[u] else KU * N

        block = ctx.enter_context(nc.Block())

        @block.sync
        def _(sp):
            sp.dma_start(ident[:], a["c_ident"]).then_inc(const_in, 16)
            for n in range(NG):
                sp.dma_start(xc(n), x_dram[:, :, N * n:N * n + N]).then_inc(x_in[n], 16)

            def load(u, src, nk, width):
                if u >= RAW:
                    sp.wait_ge(lo_done, u - RAW + 1)
                sp.dma_start(raw_slot(u % RAW, nk, width), src).then_inc(raw_in[u % RAW], 16)

            def load_units(lo, hi):
                for u in range(lo, hi):
                    d = units[u][0]
                    load(u, d.src, d.nk, d.width)

            def load_ffn(b):
                u0 = FFN[b]["u"]
                for n, (kind, q, step) in enumerate(FFN_HEAD):
                    load(u0 + n, ffn_src(b, kind, q, step), KU, N)
                with sp.Fori(0, ROUNDS) as i:
                    for n, (kind, q, ahead) in enumerate(FFN_ROUND):
                        u = u0 + len(FFN_HEAD) + n
                        sp.wait_ge(lo_done, i * 12 + (u - RAW + 1))
                        sp.dma_start(raw_slot(u % RAW, KU, N),
                                     ffn_src(b, kind, q, i + ahead)).then_inc(raw_in[u % RAW], 16)
                for n, (kind, q, step) in enumerate(FFN_TAIL):
                    load(u0 + FT_TAIL + n, ffn_src(b, kind, q, step), KU, N)

            load_units(0, RAW)
            for r, name in enumerate(VEC_ROWS[1:], 1):
                sp.dma_start(vec_rows[DK * r:DK * r + DK, :],
                             a[name][0].rearrange("(r c) -> r c", c=P)).then_inc(vec_in, 16)
            sp.dma_start(conv_rows[0:2 * FT, 0:TAPS, :],
                         a["w_ffn_conv"][0].rearrange("t (r c) -> r t c", c=P)).then_inc(vec_in, 16)
            sp.dma_start(conv_rows[0:2 * FT, TAPS, :],
                         a["b_ffn_conv"][0].rearrange("(r c) -> r c", c=P)).then_inc(vec_in, 16)
            load_units(RAW, F1)
            load_ffn(0)
            load_units(PL1, F2)
            load_ffn(1)
            load_units(PL2, UNITS)
            sp.wait_ge(out_stored, 16 * NG)

        last_unit = {d.group: u for u, x in enumerate(units) if x for d in x[:1] if d.last}
        last_unit.update({(GD1, GD2)[b] + n: (E1, E2)[b] + n for b in range(2) for n in range(NG)})

        def full(g):
            return last_unit[g] + 1

        def walk(unit_of, tasks, lo, hi, first=()):
            for u in range(lo, hi):
                now = [t for t in after.get(u, ()) if t[0] in tasks]
                for name, *args in now:
                    if name in first:
                        tasks[name](*args)
                unit_of(u)
                for name, *args in now:
                    if name not in first:
                        tasks[name](*args)

        @block.scalar
        def _(act):
            own = Own(act)

            def split(u):
                if u >= UNITS:
                    return
                act.wait_ge(raw_in[u % RAW], 16 * (u // RAW + 1))
                if u >= SPL:
                    act.wait_ge(unit_used, u - SPL + 1)
                c = columns(u)
                act.activation(w_hi[:, u % SPL, 0:c], raw[:, u % RAW, 0:c], ACT.Copy).then_inc(hi_done, 1)

            def split_at(i, u):
                act.wait_ge(raw_in[u % RAW], i * (16 * 12 // RAW) + 16 * (u // RAW + 1))
                act.wait_ge(unit_used, i * 12 + (u - SPL + 1))
                act.activation(w_hi[:, u % SPL, :], raw[:, u % RAW, :], ACT.Copy).then_inc(hi_done, 1)

            def step(func, dst, src, sem=act_step, **kw):
                act.activation(dst, src, func, **kw).then_inc(sem, 1)
                own.did(sem)

            def turn(t):
                d = turns[t]
                act.wait_ge(turn_full, t + 1)
                if d.col is None:
                    step(ACT.Copy, act_hi[d.act][:, d.k0:d.k0 + d.tiles, :],
                         aux01[:, 0:T * d.tiles].rearrange("p (f t) -> p f t", f=d.tiles), turn_hi)
                    return
                act.wait_ge(cols_done, 1)
                for k in range(d.tiles):
                    step(ACT.Copy, act_hi[d.act][:, d.k0 + k, :], fours(half_of[d.half])[:, k, :],
                         turn_hi if k == d.tiles - 1 else act_step, scale=d.col[:, k:k + 1])

            def square_pair(src, sums):
                for m in range(M):
                    if own.last is not None:
                        own.order()
                    step(ACT.Square, sq_junk, src[:, m, :], squared, accum_out=sums[:, m:m + 1])

            def square_first(n):
                act.wait_ge(x_in[n], 16)
                square_pair(xc(n), ssq1[:, n, :])

            def square_x(g, n):
                act.wait_ge(acc_free, g + 1)
                square_pair(xc(n), ssq1[:, n, :])

            def scores(p):
                act.wait_ge(max_done, 2 * p + 2)
                own.order()
                for t, lo, hi in ((0, 0, P), (1, P, P + T)):
                    for hh in range(2):
                        step(ACT.Exp, score_of(p)[:, hh, lo:hi], score_of(p)[:, hh, lo:hi], exp_done,
                             bias=mx[:, t, hh:hh + 1], accum_out=den[:, t, hh:hh + 1])

            def probs_turn(p):
                act.wait_ge(pt_full, p + 1)
                own.order()
                step(ACT.Copy, probs_of(p), aux[:, 2:4, 0:384], pt_copied)

            def weigh(p):
                act.wait_ge(o_full, p + 1)
                own.order()
                if p < 8:
                    step(ACT.Copy, act_hi[1][:, p, :], aux[:, 2, 0:T], o_hi)
                else:
                    j = 2 * (p - 8)
                    step(ACT.Copy, act_hi[0][:, j:j + 2, :], aux[:, 2, :].rearrange("p (h t) -> p h t", h=2), o_hi)

            def gate_logits(g):
                act.wait_ge(neg_abs_done, 1)
                own.order()
                step(ACT.Exp, neg_abs, neg_abs)
                own.order()
                step(ACT.Ln, neg_abs, neg_abs, log_done, bias=1.0)

            def gate_sums():
                act.wait_ge(b_full, 1)
                act.wait_ge(diff_done, 1)
                own.order()
                step(ACT.Exp, e_pos, fours(aux01), exps_done)
                step(ACT.Exp, e_neg, fours(aux01), exps_done, scale=-1.0)
                step(ACT.Exp, e_diff, e_diff, ediff_done)

            def gla_scores():
                act.wait_ge(at_full, 1)
                own.order()
                step(ACT.Copy, k_end_nat.rearrange("p m n -> p (m n)"), aux23, kend_copied)

            def gla_update01():
                act.wait_ge(upd_full, 1)
                own.order()
                step(ACT.Copy, states[:, 0, :, :], fours(aux01), state_first)

            def gla_squares(m):
                act.wait_ge(og_full, m + 1)
                for h in range(GH):
                    own.order()
                    step(ACT.Square, e_neg[:, 0, :], fours((aux23, aux01)[m])[:, h, :], og_sq,
                         accum_out=ssh[:, GH * m + h:GH * m + h + 1])

            def r_gate(g):
                act.wait_ge(acc_free, 12 + g)
                own.order()
                step(ACT.Silu, gla_r[:, :, N * g:N * g + N], gla_r[:, :, N * g:N * g + N], r_silu)

            def ffn_a(b, it, part, freed):
                if b == 0:
                    act.wait_ge(acc_free, freed)
                    own.order()
                    for f in range(KU):
                        step(ACT.Identity, (f_gate, f_val)[part][:, f, :], up_in[:, f, TAPS - 1:TAPS - 1 + T], conv_a,
                             scale=conv_now[:, TAPS - 1, part, f:f + 1], bias=conv_now[:, TAPS, part, f:f + 1])

            def ffn_act(b, it, freed):
                if b == 0:
                    act.wait_ge(conv_b, it * 8 + 4)
                else:
                    act.wait_ge(acc_free, freed)
                own.order()
                step(ACT.Gelu_apprx_tanh if b == 0 else ACT.Silu, f_gate, f_gate, act_f)

            def ffn_c(b, it, tile=0):
                f = FFN[b]
                act.wait_ge(f_full, it + (f["it0"] + 1))
                own.order()
                step(ACT.Copy, act_hi[f["f_act"]][:, tile:tile + KU, :], f_val, f_hi)

            def ffn(b):
                f = FFN[b]
                u0, g0 = f["u"], f["g"]
                last = FS - 1
                head = {3: lambda: ffn_a(b, 0, 0, g0 + 1), 5: lambda: ffn_act(b, 0, g0 + 1),
                        7: lambda: ffn_a(b, 0, 1, g0 + 2)}
                for j in range(8):
                    split(u0 + j + SPL)
                    for name, *args in after.get(u0 + j, ()):
                        if name in tasks:
                            tasks[name](*args)
                    if j in head:
                        head[j]()
                own.order()
                with act.Fori(0, ROUNDS) as i:
                    end = conv_a if b == 0 else act_f
                    own.enter(i, [(act_f, 1), (f_hi, 1)] + [(conv_a, 8)] * (b == 0), end)
                    for j in range(12):
                        split_at(i, u0 + 8 + j + SPL)
                        if j == 1:
                            ffn_c(b, i)
                        if j == 3:
                            ffn_a(b, i + 1, 0, i * 6 + (g0 + 3))
                        if j == 9:
                            ffn_act(b, i + 1, i * 6 + (g0 + 3))
                        if j == 11:
                            ffn_a(b, i + 1, 1, i * 6 + (g0 + 8))
                    own.leave(ROUNDS, end)
                gt = g0 + G_TAIL
                tail = {1: lambda: ffn_c(b, last - 1), 3: lambda: ffn_a(b, last, 0, gt + 1),
                        5: lambda: ffn_act(b, last, gt + 1), 7: lambda: ffn_a(b, last, 1, gt + 2),
                        9: lambda: ffn_c(b, last, KU)}
                for j in range(12):
                    split(u0 + FT_TAIL + j + SPL)
                    if j in tail:
                        tail[j]()

            def ple_gate(g, n, b):
                act.wait_ge(acc_free, g + 1)
                own.order()
                step(ACT.Sigmoid, ple_t, ple_t, sig_done)

            def ple_add(g, n, b):
                if b == 0:
                    act.wait_ge(x_fresh, 2 * n + 1)
                    square_pair(ple_t, ssq1[:, n, :])
                    act.wait_ge(x_fresh, 2 * n + 2)
                    square_pair(xc(n), ssq2[:, n, :])

            def rope_square(g, q, kind, h):
                if kind[0] == "a":
                    act.wait_ge(acc_free, g + 1)
                    own.order()
                    step(ACT.Square, z1, z, z_sq)

            def qk_copy(q, dst):
                if q == 0:
                    act.wait_ge(x_stored, 16 * NG)
                act.wait_ge(qk_full, q + 1)
                own.order()
                step(ACT.Copy, dst, fours(aux01), qk_copied)

            def ret_gate(h):
                act.wait_ge(acc_free, G_W2 + (10, 14)[h])
                own.order()
                step(ACT.Silu, ret_g[h], ret_g[h], r_silu)

            def ret_scores(h):
                act.wait_ge(s_full, h + 1)
                own.order()
                step(ACT.Copy, k_dec[h], aux[:, 2, :], s_state)

            def ret_out(h):
                act.wait_ge(ret_full, h + 1)
                own.order()
                step(ACT.Square, half_k[h], fours(aux23), og_sq)

            tasks = dict(turn=turn, square_first=square_first, square_x=square_x, scores=scores,
                         probs_turn=probs_turn, weigh=weigh, gate_logits=gate_logits, gate_sums=gate_sums, gla_scores=gla_scores,
                         gla_update01=gla_update01, gla_out0=lambda: gla_squares(0), gla_out1=lambda: gla_squares(1),
                         r_gate=r_gate, ple_gate=ple_gate, ple_add=ple_add, rope=rope_square, qk_turn=qk_copy,
                         ret_gate=ret_gate, ret_scores=ret_scores, ret_out=ret_out)
            act.dma_start(vec_rows[0:DK, :], a[VEC_ROWS[0]][0].rearrange("(r c) -> r c", c=P)).then_inc(mix_in, 16)
            walk(lambda u: split(u + SPL) if u >= -SPL else None, tasks, -SPL - 1, F1)
            ffn(0)
            walk(lambda u: split(u + SPL), tasks, PL1 - 4, F2)
            ffn(1)
            walk(lambda u: split(u + SPL), tasks, PL2 - 4, UNITS)

        @block.vector
        def _(v):
            own = Own(v)

            def remainder(u):
                if u >= UNITS:
                    return
                v.wait_ge(hi_done, u + 1)
                c = columns(u)
                v.tensor_tensor(w_lo[:, u % SPL, 0:c], raw[:, u % RAW, 0:c], w_hi[:, u % SPL, 0:c],
                                ALU.subtract).then_inc(lo_done, 1)

            def remainder_at(i, u):
                v.wait_ge(hi_done, i * 12 + (u + 1))
                v.tensor_tensor(w_lo[:, u % SPL, :], raw[:, u % RAW, :], w_hi[:, u % SPL, :],
                                ALU.subtract).then_inc(lo_done, 1)

            def did(sem=vec_step):
                own.did(sem)

            def turn(t):
                d = turns[t]
                v.wait_ge(turn_hi, t + 1)
                own.order()
                lo, hi = act_lo[d.act], act_hi[d.act]
                if d.col is None:
                    at = slice(d.k0, d.k0 + d.tiles)
                    v.tensor_tensor(lo[:, at, :], aux01[:, 0:T * d.tiles].rearrange("p (f t) -> p f t", f=d.tiles),
                                    hi[:, at, :], ALU.subtract).then_inc(turned, 1)
                    did(turned)
                    return
                for k in range(d.tiles):
                    s = turned if k == d.tiles - 1 else vec_step
                    v.scalar_tensor_tensor(lo[:, d.k0 + k, :], fours(half_of[d.half])[:, k, :], d.col[:, k:k + 1],
                                           hi[:, d.k0 + k, :].bitcast(F32), ALU.mult, ALU.subtract).then_inc(s, 1)
                    did(s)

            def norm_sums(k):
                v.wait_ge(squared, (8, 16, 24, 40, 48, 56)[k])
                own.order()
                v.tensor_reduce(mean1, ssq1.rearrange("p n m -> p m n"), AX_X, ALU.add).then_inc(vec_step, 1)
                did()
                own.order()
                v.tensor_scalar(mean1, mean1, 1.0 / D, EPS, ALU.mult, ALU.add).then_inc(mean_done, 1)
                did(mean_done)

            def norm_diag(k):
                v.wait_ge(r_done, (1, 2, 5)[k])
                if k == 0:
                    v.wait_ge(const_in, 16)
                own.order()
                for m in range(M):
                    v.tensor_scalar(diag[:, P * m:P * m + P], ident[:], r_col[:, m:m + 1], None,
                                    ALU.mult).then_inc(diag_done, 1)
                    did(diag_done)

            def norm_row(k):
                v.wait_ge(row_full, k + 1)
                own.order()
                v.tensor_copy(r_row[:], aux[:, 2, 0:T]).then_inc(row_done, 1)
                did(row_done)
                if k == 1:
                    v.memset(up_in[:, :, 0:TAPS - 1], 0.0).then_inc(vec_step, 1)
                    did()

            def tables():
                v.wait_ge(cols_full, 2)
                v.tensor_copy(vec_cols[:, DK:6 * DK], aux[:, 3, 8 * FT + DK:8 * FT + 6 * DK]).then_inc(vec_step, 1)
                did()
                v.tensor_copy(conv_cols[:].rearrange("p t s f -> p (t s f)"),
                              aux[:, 3, 0:8 * FT]).then_inc(cols_done, 1)
                did(cols_done)

            def final_sums():
                norm_sums(3)
                own.order()
                v.tensor_reduce(mean2, ssq2.rearrange("p n m -> p m n"), AX_X, ALU.add).then_inc(vec_step, 1)
                did()
                own.order()
                v.tensor_scalar(mean2, mean2, 1.0 / D, None, ALU.mult).then_inc(vec_step, 1)
                did()
                own.order()
                v.scalar_tensor_tensor(mean2, mean1, EPS, mean2, ALU.mult, ALU.add).then_inc(mean_done, 1)
                did(mean_done)

            def evac(g, dst):
                v.wait_ge(unit_used, full(g))
                v.wait_ge(r_done, 1 if g < 13 else 3 if g < G_W2 else 4)
                own.order()
                for m in range(M):
                    s = acc_free if m == M - 1 else vec_step
                    v.tensor_scalar(dst[:, m, :], acc[:, g % 2, m, :], r_col[:, m:m + 1], None,
                                    ALU.mult).then_inc(s, 1)
                    did(s)

            def evac_flipped(g, dst, value=None):
                v.wait_ge(unit_used, full(g) if value is None else value)
                own.order()
                v.tensor_tensor(dst, fours(acc[:, g % 2, :, :].rearrange("p b n -> p (b n)")),
                                r_row[:].unsqueeze(1).to_broadcast([P, KU, T]), ALU.mult).then_inc(acc_free, 1)
                did(acc_free)

            def residual(g, n, how):
                v.wait_ge(unit_used, full(g))
                if how != 1 and n == 0:
                    v.wait_ge(x_back, 16 * (1 + (how == 2)))
                own.order()
                if how < 2:
                    v.tensor_tensor(xc(n), acc[:, g % 2, :, :], xc(n), ALU.add).then_inc(acc_free, 1)
                    did(acc_free)
                    return
                for m in range(M):
                    s = acc_free if m == M - 1 else vec_step
                    v.scalar_tensor_tensor(xc(n)[:, m, :], xc(n)[:, m, :], r_final[:, m:m + 1],
                                           acc[:, g % 2, m, :], ALU.mult, ALU.add).then_inc(s, 1)
                    did(s)

            def scores(p):
                v.wait_ge(scores_full, p + 1)
                if p < 8:
                    b = bias[p % 2]
                    v.wait_ge(bias_in[p % 2], 16 * (p // 2 + 1))
                    own.order()
                    v.memset(b[0:CH, :, 0:CH], NEG).then_inc(vec_step, 1)
                    did()
                    both = (b[:, :, P - 1::-1], b[:, :, T - 1::-1])
                    scale = AHD ** -0.5
                else:
                    v.wait_ge(tab_in, 16 * 6)
                    both = (causal[:, P:T].unsqueeze(1).to_broadcast([P, 2, P]),
                            causal[:].unsqueeze(1).to_broadcast([P, 2, T]))
                    scale = HD ** -0.5
                own.order()
                for t, lo, hi in ((0, 0, P), (1, P, P + T)):
                    v.scalar_tensor_tensor(score_of(p)[:, :, lo:hi], aux[:, 0:2, lo:hi], scale, both[t],
                                           ALU.mult, ALU.add).then_inc(biased, 1)
                    did(biased)
                own.order()
                for t, lo, hi in ((0, 0, P), (1, P, P + T)):
                    v.tensor_reduce(mx[:, t, :], score_of(p)[:, :, lo:hi], AX_X, ALU.max,
                                    negate=True).then_inc(max_done, 1)
                    did(max_done)

            def normalise(p):
                v.wait_ge(exp_done, 4 * p + 4)
                own.order()
                v.reciprocal(rden, den).then_inc(vec_step, 1)
                did()
                own.order()
                for t, lo, hi in ((0, 0, P), (1, P, P + T)):
                    for hh in range(2):
                        part = score_of(p)[:, hh, lo:hi]
                        v.tensor_scalar(part, part, rden[:, t, hh:hh + 1], None, ALU.mult).then_inc(probs_done, 1)
                        did(probs_done)

            def weigh(p):
                v.wait_ge(o_hi, p + 1)
                own.order()
                if p < 8:
                    dst, src, hi = act_lo[1][:, p, :], aux[:, 2, 0:T], act_hi[1][:, p, :]
                else:
                    j = 2 * (p - 8)
                    dst, hi = act_lo[0][:, j:j + 2, :], act_hi[0][:, j:j + 2, :]
                    src = aux[:, 2, :].rearrange("p (h t) -> p h t", h=2)
                v.tensor_tensor(dst, src, hi, ALU.subtract).then_inc(o_done, 1)
                did(o_done)

            def rank_out(g):
                v.wait_ge(unit_used, full(g))
                own.order()
                v.memset(glr_t[0:RANK + 1, :], 1.0).then_inc(vec_step, 1)
                did()
                own.order()
                v.tensor_tensor(glr_t[0:RANK, :], acc[0:RANK, g % 2, 0, 0:T], r_row[0:RANK, :],
                                ALU.mult).then_inc(glr_copied, 1)
                did(glr_copied)

            def gate_logits(g):
                v.wait_ge(logits_full, 1)
                own.order()
                v.tensor_scalar(neg_part, acc[:, g % 2, :, :], 0.0, None, ALU.min).then_inc(vec_step, 1)
                did()
                v.tensor_scalar(log_a, acc[:, g % 2, :, :], 0.0, None, ALU.max).then_inc(acc_free, 1)
                did(acc_free)
                own.order()
                v.tensor_tensor(neg_abs, neg_part, log_a, ALU.subtract).then_inc(neg_abs_done, 1)
                did(neg_abs_done)

            def gate_logs():
                v.wait_ge(log_done, 1)
                own.order()
                v.tensor_tensor(log_a, neg_part, neg_abs, ALU.subtract).then_inc(log_a_done, 1)
                did(log_a_done)

            def gate_sums():
                v.wait_ge(b_full, 1)
                own.order()
                ends = aux01.rearrange("p (h i) -> p h i", i=CH)[:, :, CH - 1]
                v.tensor_copy(decay_cols, ends).then_inc(vec_step, 1)
                did()
                own.order()
                v.tensor_tensor(e_diff.rearrange("p h (c i) -> p (h c) i", i=CH),
                                decay_cols.unsqueeze(2).to_broadcast([P, 16, CH]),
                                aux01.rearrange("p (h i) -> p h i", i=CH), ALU.subtract).then_inc(diff_done, 1)
                did(diff_done)

            def decay():
                v.wait_ge(exps_done, 2)
                own.order()
                v.scalar_tensor_tensor(gla_q, gla_q, GDK ** -0.5, e_pos, ALU.mult, ALU.mult).then_inc(decayed, 1)
                did(decayed)
                v.tensor_tensor(e_neg, gla_k, e_neg, ALU.mult).then_inc(decayed, 1)
                did(decayed)
                v.wait_ge(ediff_done, 1)
                own.order()
                v.tensor_tensor(gla_k, gla_k, e_diff, ALU.mult).then_inc(decayed, 1)
                did(decayed)

            def gla_scores():
                v.memset(gla_at, 0.0).then_inc(vec_step, 1)
                did()
                v.wait_ge(at_full, 1)
                own.order()
                v.wait_ge(gla_in, 32)
                v.copy_predicated(gla_at, chunk_mask.bitcast(U32).unsqueeze(1).to_broadcast([P, 2 * GH, P]),
                                  aux01.rearrange("p (h i) -> p h i", i=P)).then_inc(at_done, 1)
                did(at_done)

            def carry(c, src):
                for h in range(GH):
                    v.scalar_tensor_tensor(states[:, c, h, :], states[:, c - 1, h, :],
                                           e_pos[:, h, CH * c + CH - 1:CH * c + CH],
                                           fours(src)[:, h, :], ALU.mult, ALU.add).then_inc(state_done, 1)
                    did(state_done)

            def gla_update01():
                v.wait_ge(state_first, 1)
                v.wait_ge(upd_full, 1)
                own.order()
                carry(1, aux23)

            def gla_update2():
                v.wait_ge(upd_full, 2)
                own.order()
                carry(2, aux01)

            def r_gate(g):
                v.wait_ge(r_silu, g + 1)
                v.wait_ge(gla_in, 48)
                own.order()
                part = gla_r[:, :, N * g:N * g + N].rearrange("p m (h e) -> p m h e", e=GDV)
                for m in range(M):
                    v.tensor_tensor(part[:, m], part[:, m], w_row[:].unsqueeze(1).to_broadcast([P, 2, GDV]),
                                    ALU.mult).then_inc(vec_step, 1)
                    did()

            def head_factors(count, width):
                own.order()
                v.tensor_scalar(ssh, ssh, 1.0 / width, EPS, ALU.mult, ALU.add).then_inc(z_sum, 1)
                did(z_sum)
                v.wait_ge(z_r, count)

            def gla_norm():
                v.wait_ge(og_sq, 8)
                head_factors(1, GDV)
                own.order()
                for m in range(M):
                    for h in range(GH):
                        s = yg_done if (m, h) == (M - 1, GH - 1) else vec_step
                        part = gla_r[:, m, GDV * h:GDV * h + GDV]
                        v.scalar_tensor_tensor(part, fours((aux23, aux01)[m])[:, h, :],
                                               rr[:, GH * m + h:GH * m + h + 1], part,
                                               ALU.mult, ALU.mult).then_inc(s, 1)
                        did(s)

            def ffn_a(b, it, part, g, value):
                if b == 1:
                    evac_flipped(g, (f_gate, f_val)[part], value)
                    return
                if part == 0:
                    own.order()
                    at = slice(it * KU, it * KU + KU) if isinstance(it, int) else bass.ds(it * KU, KU)
                    v.tensor_copy(conv_now[:], conv_cols[:, :, :, at]).then_inc(vec_step, 1)
                    did()
                evac_flipped(g, up_in[:, :, TAPS - 1:TAPS - 1 + T], value)

            def ffn_b(b, it, part):
                if b == 1:
                    return
                dst = (f_gate, f_val)[part]
                v.wait_ge(conv_a, it * 8 + 4 * (part + 1))
                own.order()
                for tap in (1, 0):
                    for f in range(KU):
                        s = vec_step if tap else conv_b
                        v.scalar_tensor_tensor(dst[:, f, :], up_in[:, f, tap:tap + T],
                                               conv_now[:, tap, part, f:f + 1], dst[:, f, :],
                                               ALU.mult, ALU.add).then_inc(s, 1)
                        did(s)
                    if tap:
                        own.order()

            def ffn_c(b, it):
                v.wait_ge(act_f, it + (FFN[b]["it0"] + 1))
                own.order()
                v.tensor_tensor(f_val, f_gate, f_val, ALU.mult).then_inc(f_full, 1)
                did(f_full)

            def ffn_d(b, it, tile=0):
                f = FFN[b]
                v.wait_ge(f_hi, it + (f["it0"] + 1))
                own.order()
                at = slice(tile, tile + KU)
                v.tensor_tensor(act_lo[f["f_act"]][:, at, :], f_val, act_hi[f["f_act"]][:, at, :],
                                ALU.subtract).then_inc(f_done, 1)
                did(f_done)

            def add_down(g, n, value):
                v.wait_ge(unit_used, value)
                own.order()
                v.tensor_tensor(xc(n), acc[:, g % 2, :, :], xc(n), ALU.add).then_inc(acc_free, 1)
                did(acc_free)

            def ffn(b):
                f = FFN[b]
                u0, g0 = f["u"], f["g"]
                last = FS - 1
                head = {3: lambda: ffn_a(b, 0, 0, g0, u0 + 4), 4: lambda: ffn_b(b, 0, 0),
                        7: lambda: ffn_a(b, 0, 1, g0 + 1, u0 + 8)}

                def slot(u):
                    head.get(u - u0, lambda: None)()
                    remainder(u + SPL)

                walk(slot, tasks, u0, u0 + 8, first)
                own.order()
                with v.Fori(0, ROUNDS) as i:
                    per = [(acc_free, 6), (f_full, 1), (f_done, 1)] + [(vec_step, 9), (conv_b, 8)] * (b == 0)
                    own.enter(i, per, acc_free)
                    for j in range(12):
                        if j == 0:
                            ffn_b(b, i, 1)
                        if j == 1:
                            ffn_c(b, i)
                        if j == 2:
                            ffn_d(b, i)
                        if j == 3:
                            ffn_a(b, i + 1, 0, g0 + 2, i * 12 + (u0 + 12))
                        if 4 <= j < 8:
                            add_down(g0 + j - 1, j - 4, i * 12 + (u0 + 8 + j + 1))
                        if j == 8:
                            ffn_b(b, i + 1, 0)
                        if j == 11:
                            ffn_a(b, i + 1, 1, g0 + 7, i * 12 + (u0 + 20))
                        remainder_at(i, u0 + 8 + j + SPL)
                    own.leave(ROUNDS, acc_free)
                ut, gt = u0 + FT_TAIL, g0 + G_TAIL
                tail = {0: lambda: ffn_b(b, last - 1, 1), 1: lambda: ffn_c(b, last - 1), 2: lambda: ffn_d(b, last - 1),
                        3: lambda: ffn_a(b, last, 0, gt, ut + 4), 4: lambda: ffn_b(b, last, 0),
                        7: lambda: ffn_a(b, last, 1, gt + 1, ut + 8)}
                for j in range(12):
                    if j in tail:
                        tail[j]()
                    if j >= 8:
                        add_down(gt + j - 6, j - 8, ut + j + 1)
                        if j == 8:
                            ffn_b(b, last, 1)
                        if j == 9:
                            ffn_c(b, last)
                        if j == 10:
                            ffn_d(b, last, KU)
                    remainder(ut + j + SPL)

            def ple_gate(g, n, b):
                if b == 0 and n:
                    v.wait_ge(squared, 24 + 4 * n)
                v.wait_ge(unit_used, full(g))
                v.wait_ge(r_done, 3 if b == 0 else 6)
                own.order()
                if b:
                    v.wait_ge(ple_tab[b], 16)
                for m in range(M):
                    s = acc_free if m == M - 1 else vec_step
                    if b == 0:
                        v.tensor_scalar(ple_t[:, m, :], acc[:, g % 2, m, :], r_col[:, m:m + 1], None,
                                        ALU.mult).then_inc(s, 1)
                    else:
                        v.scalar_tensor_tensor(ple_t[:, m, :], acc[:, g % 2, m, :], r_col[:, m:m + 1],
                                               wf_b[:, N * n:N * n + N], ALU.mult, ALU.add).then_inc(s, 1)
                    did(s)

            def ple_add(g, n, b):
                v.wait_ge(sig_done, NG * b + n + 1)
                v.wait_ge(unit_used, full(g))
                own.order()
                v.tensor_tensor(ple_t, acc[:, g % 2, :, :], ple_t, ALU.mult).then_inc(acc_free, 1)
                did(acc_free)
                own.order()
                if b:
                    v.tensor_tensor(xc(n), ple_t, xc(n), ALU.add).then_inc(x_fresh, 1)
                    did(x_fresh)
                    return
                v.tensor_tensor(ple_t, ple_t, xc(n), ALU.add).then_inc(x_fresh, 1)
                did(x_fresh)
                v.wait_ge(ple_tab[b], 16)
                own.order()
                v.tensor_tensor(xc(n), ple_t, wf_b[:, N * n:N * n + N].unsqueeze(1).to_broadcast([P, M, N]),
                                ALU.mult).then_inc(x_fresh, 1)
                did(x_fresh)

            def swapped(src):
                return src.rearrange("p (h s e) -> p h s e", s=2, e=HD // 2)[:, :, ::-1, :]

            def rope_tables():
                v.wait_ge(tab_in, 16 * 6)
                own.order()
                for kind in (1, 0):
                    w = w_row[:, HD * kind:HD * kind + HD]
                    other = w.rearrange("p (s e) -> p s e", s=2)[:, ::-1, :]
                    for m in range(M):
                        v.tensor_tensor(rope[kind][:, m, 0, :], rope[0][:, m, 0, :], w, ALU.mult).then_inc(vec_step, 1)
                        did()
                        v.tensor_tensor(rope[kind][:, m, 1, :].rearrange("p (s e) -> p s e", s=2),
                                        rope[0][:, m, 1, :].rearrange("p (s e) -> p s e", s=2),
                                        other, ALU.mult).then_inc(vec_step, 1)
                        did()
                    own.order()

            def rope_in(g, q):
                if q == 0:
                    v.wait_ge(x_stored, 16 * NG)
                if q:
                    v.wait_ge(qk_full, q)
                evac(g, z)

            def rope_group(g, q, kind, h):
                if q == 0:
                    rope_tables()
                own.order()
                if kind[0] == "a":
                    v.wait_ge(z_sq, (0, 1, 2, 3)[q] + 1)
                    v.tensor_reduce(ssh, z1.rearrange("p m (h e) -> p (m h) e", e=HD), AX_X,
                                    ALU.add).then_inc(vec_step, 1)
                    did()
                    head_factors(2 + q, HD)
                    own.order()
                tab = rope[2] if kind[0] == "r" else rope["qk".index(kind[1])]
                four = lambda x, m: x[:, m, :].rearrange("p (h e) -> p h e", e=HD)
                for m in range(M):
                    v.tensor_tensor(four(z1, m), four(z, m), tab[:, m, 0, :].unsqueeze(1).to_broadcast([P, 4, HD]),
                                    ALU.mult).then_inc(vec_step, 1)
                    did()
                    sine = tab[:, m, 1, :].rearrange("p (s e) -> p s e", s=2)
                    sine = sine.unsqueeze(1).to_broadcast([P, 4, 2, HD // 2])
                    v.tensor_tensor(z2[:, m, :].rearrange("p (h s e) -> p h s e", s=2, e=HD // 2), swapped(z[:, m, :]),
                                    sine, ALU.mult).then_inc(vec_step, 1)
                    did()
                own.order()
                s = vec_step if kind[0] == "a" else roped
                v.tensor_tensor(z1, z1, z2, ALU.add).then_inc(s, 1)
                did(s)
                if kind[0] == "a":
                    own.order()
                    eight = z1.rearrange("p m (h e) -> p (m h) e", e=HD)
                    v.tensor_tensor(eight, eight, rr.unsqueeze(2).to_broadcast([P, 8, HD]), ALU.mult).then_inc(roped, 1)
                    did(roped)
                if kind == "rk":
                    own.order()
                    v.tensor_tensor(k_dec[h].rearrange("p (h e) -> p h e", e=HD), four(z1, 0),
                                    k_decay[:, 4 * h:4 * h + 4].unsqueeze(2).to_broadcast([P, 4, HD]),
                                    ALU.mult).then_inc(vec_step, 1)
                    did()

            def ret_gate(h):
                v.wait_ge(r_silu, 3 + h)
                v.wait_ge(ret_tab_in, 48 * (h + 1))
                own.order()
                v.tensor_tensor(ret_g[h], ret_g[h], g_ret.unsqueeze(1).to_broadcast([P, M, N]),
                                ALU.mult).then_inc(vec_step, 1)
                did()

            def ret_scores(h):
                v.wait_ge(s_full, h + 1)
                own.order()
                v.tensor_tensor(half_k[h].rearrange("p h (m i) -> p h m i", m=M),
                                aux01.rearrange("p (h m i) -> p h m i", h=4, m=M),
                                decay_m.unsqueeze(2).to_broadcast([P, 4, M, P]), ALU.mult).then_inc(s_decayed, 1)
                did(s_decayed)
                v.tensor_tensor(half_q[h][:, :, P:T], half_q[h][:, :, P:T], q_decay, ALU.mult).then_inc(s_decayed, 1)
                did(s_decayed)

            def ret_out(h):
                v.wait_ge(og_sq, 9 + h)
                own.order()
                v.tensor_reduce(ssh, half_k[h].rearrange("p h (s e) -> p (h s) e", e=HD), AX_X,
                                ALU.add).then_inc(vec_step, 1)
                did()
                head_factors(6 + h, HD)
                own.order()
                for m in range(M):
                    for n in range(4):
                        s = yg_done if (m, n) == (M - 1, 3) else vec_step
                        part = ret_g[h][:, m, HD * n:HD * n + HD]
                        v.scalar_tensor_tensor(part, aux[:, 2 + m, HD * n:HD * n + HD], rr[:, 4 * m + n:4 * m + n + 1],
                                               part, ALU.mult, ALU.mult).then_inc(s, 1)
                        did(s)

            tasks = dict(turn=turn, norm_sums=norm_sums, norm_diag=norm_diag, norm_row=norm_row,
                         tables=tables, gate_logs=gate_logs, decay=decay, rope_in=rope_in,
                         final_sums=final_sums, evac=evac,
                         evac_flipped=evac_flipped, residual=residual, scores=scores, normalise=normalise,
                         weigh=weigh, rank_out=rank_out, gate_logits=gate_logits,
                         gate_sums=gate_sums, gla_scores=gla_scores, gla_update01=gla_update01,
                         gla_update2=gla_update2, r_gate=r_gate, gla_norm=gla_norm, ple_gate=ple_gate,
                         ple_add=ple_add, rope=rope_group, ret_gate=ret_gate, ret_scores=ret_scores,
                         ret_out=ret_out)
            first = {"evac", "evac_flipped", "residual", "norm_sums", "norm_diag", "norm_row", "tables",
                     "scores", "normalise", "rank_out", "gate_logits", "gate_logs", "gate_sums",
                     "decay", "gla_scores", "gla_update01", "gla_update2", "ple_gate", "ple_add", "rope_in",
                     "ret_scores"}
            v.memset(ones[:], 1.0).then_inc(vec_step, 1)
            did()
            v.memset(half_neg, -0.5).then_inc(ones_done, 1)
            did(ones_done)
            v.wait_ge(cols_full, 1)
            v.tensor_copy(vec_cols[:, 0:DK], aux[:, 2, 0:DK]).then_inc(cols_done, 1)
            did(cols_done)
            walk(lambda u: remainder(u + SPL) if u >= -SPL else None, tasks, -SPL - 1, F1, first)
            ffn(0)
            walk(lambda u: remainder(u + SPL), tasks, PL1 - 4, F2, first)
            ffn(1)
            walk(lambda u: remainder(u + SPL), tasks, PL2 - 4, UNITS, first)

        @block.tensor
        def _(pe):
            read = {"01": [], "23": [(cols_done, 1)]}

            def free(half, *read_by):
                for s, n in read[half]:
                    pe.wait_ge(s, n)
                read[half] = list(read_by)

            def products(act_b, k, wk, u, flipped, s, width, start, stop):
                xh, xl = act_hi[act_b], act_lo[act_b]
                wh = w_hi[:, u % SPL, wk * width:wk * width + width]
                wl = w_lo[:, u % SPL, wk * width:wk * width + width]
                mm = None
                if flipped:
                    flat = acc[:, s, :, :].rearrange("p b n -> p (b n)")
                    rows = min(width, P)
                    for f in range(width // rows):
                        c = slice(rows * f, rows * f + rows)
                        for n, (w, x) in enumerate(((wh, xh), (wh, xl), (wl, xh))):
                            mm = pe.matmul(flat[0:rows, T * f:T * f + T], w[:, c], x[:, k, :],
                                           start=start and n == 0 and f % 2 == 0, stop=stop and n == 2,
                                           skip_group_check=True)
                else:
                    for m in range(M):
                        c = slice(P * m, P * m + P)
                        for n, (x, w) in enumerate(((xh, wh), (xh, wl), (xl, wh))):
                            mm = pe.matmul(acc[:, s, m, 0:width], x[:, k, c], w, start=start and n == 0,
                                           stop=stop and n == 2, skip_group_check=True)
                return mm

            def multiply(u):
                d, needs = units[u]
                for s, n in needs:
                    pe.wait_ge(s, n)
                if d.first and d.group >= 2:
                    pe.wait_ge(acc_free, d.group - 1)
                pe.wait_ge(lo_done, u + 1)
                for k in range(d.nk):
                    last = k == d.nk - 1
                    mm = products(d.act, d.k0 + k, k, u, d.flipped, d.group % 2,
                                  d.width, d.first and k == 0, d.last and last)
                mm.then_inc(unit_used, 1)

            def turn(t):
                d = turns[t]
                pe.wait_ge(*d.ready)
                free(d.half, (turned, t + 1), (turn_hi, t + 1))
                for k in range(d.tiles):
                    for m in range(M):
                        mm = pe.transpose(half_of[d.half][:, T * k + P * m:T * k + P * m + P],
                                          d.src[:, m, P * k:P * k + P], ident[:])
                mm.then_inc(turn_full, 1)

            def tables():
                pe.wait_ge(vec_in, 16 * (len(VEC_ROWS) + 1))
                free("23", (cols_done, 2))
                n = DK * len(VEC_ROWS)
                pe.transpose(aux[:, 3, 8 * FT:8 * FT + n], vec_rows[0:n, :], ident[0:n, 0:n])
                for t in range(TAPS + 1):
                    mm = pe.transpose(aux[:, 3, 2 * FT * t:2 * FT * t + 2 * FT], conv_rows[0:2 * FT, t, :],
                                      ident[0:2 * FT, 0:2 * FT])
                mm.then_inc(cols_full, 1)

            def norm_row(k):
                pe.wait_ge(diag_done, 2 * k + 2)
                pe.wait_ge(ones_done, 1)
                free("23", (row_done, k + 1))
                pe.matmul(aux[:, 2, 0:T], ones[:], diag[:], start=True, stop=True).then_inc(row_full, 1)

            def scores(p):
                if p < 8:
                    pe.wait_ge(acc_free, 3 * (p // 4) + 2)
                else:
                    pe.wait_ge(qk_copied, 2 * ((p - 8) // 2) + 2)
                free("01", (biased, 2 * p + 2))
                for hh in range(2):
                    if p < 8:
                        rows = slice(AHD * hh, AHD * hh + AHD)
                        q, k = att_q[p // 4][rows, p % 4, :], att_k[p // 4][rows, p % 4, :]
                    else:
                        h, n = (p - 8) // 2, 2 * (p % 2) + hh
                        q, k = half_q[h][:, n, :], half_k[h][:, n, :]
                    pe.matmul(aux[:, hh, 0:P], q[:, 0:P], k[:, 0:P], start=True, stop=True)
                    mm = pe.matmul(aux[:, hh, P:P + T], q[:, P:T], k, start=True, stop=True)
                mm.then_inc(scores_full, 1)

            def probs_turn(p):
                pe.wait_ge(probs_done, 4 * p + 4)
                free("23", (pt_copied, p + 1))
                for hh in range(2):
                    for n in range(3):
                        c = slice(P * n, P * n + P)
                        mm = pe.transpose(aux[:, 2 + hh, c], score_of(p)[:, hh, c], ident[:])
                mm.then_inc(pt_full, 1)

            def weigh(p):
                if p < 8:
                    pe.wait_ge(acc_free, 3 * (p // 4) + 3)
                else:
                    pe.wait_ge(acc_free, G_W2 + 3 * ((p - 8) // 2) + 3)
                free("23", (o_done, p + 1), (o_hi, p + 1))
                pt = probs_of(p)
                for hh in range(2):
                    if p < 8:
                        out_ap = aux[AHD * hh:AHD * hh + AHD, 2, 0:T]
                        c = slice(P * (p % 4) + AHD * hh, P * (p % 4) + AHD * hh + AHD)
                        vals = att_v[p // 4]
                    else:
                        out_ap = aux[:, 2, T * hh:T * hh + T]
                        n = 2 * (p % 2) + hh
                        c, vals = slice(HD * n, HD * n + HD), half_v[(p - 8) // 2]
                    pe.matmul(out_ap, vals[:, 0, c], pt[:, hh, 0:T], start=True, stop=False, skip_group_check=True)
                    mm = pe.matmul(out_ap[:, P:T], vals[:, 1, c], pt[:, hh, T:T + P], start=False, stop=True,
                                   skip_group_check=True)
                mm.then_inc(o_full, 1)

            def gate_logits(g):
                pe.wait_ge(glr_copied, 1)
                pe.wait_ge(small_in, 32)
                for m in range(M):
                    mm = pe.matmul(acc[:, g % 2, m, :], glr_t[0:RANK + 1, P * m:P * m + P], up_aug[0:RANK + 1, :],
                                   start=True, stop=True)
                mm.then_inc(logits_full, 1)

            def gate_sums():
                pe.wait_ge(log_a_done, 1)
                pe.wait_ge(gla_in, 48)
                free("01", (exps_done, 2), (diff_done, 1))
                for h in range(GH):
                    for m in range(M):
                        mm = pe.matmul(fours(aux01)[:, h, P * m:P * m + P], log_a[:, m, GDK * h:GDK * h + GDK],
                                       cumsum_m, start=True, stop=True, skip_group_check=True)
                mm.then_inc(b_full, 1)

            def gla_scores():
                pe.wait_ge(decayed, 3)
                free("01", (at_done, 1))
                free("23", (kend_copied, 1))
                for h in range(GH):
                    for m in range(M):
                        c = slice(P * m, P * m + P)
                        pe.matmul(fours(aux01)[:, h, c], e_neg[:, h, c], gla_q[:, h, c], start=True, stop=True,
                                  skip_group_check=True)
                        mm = pe.transpose(aux[:, 2 + m, P * h:P * h + P], gla_k[:, h, c], ident[:])
                mm.then_inc(at_full, 1)

            def update(c, dst):
                rows = slice(CH * (c % 2), CH * (c % 2) + CH)
                for h in range(GH):
                    mm = pe.matmul(fours(dst)[:, h, :], k_end_nat[rows, c // 2, GDK * h:GDK * h + GDK],
                                   gla_v[rows, c // 2, GDV * h:GDV * h + GDV], start=True, stop=True,
                                   skip_group_check=True)
                return mm

            def gla_update01():
                pe.wait_ge(kend_copied, 1)
                pe.wait_ge(acc_free, 11)
                free("01", (state_first, 1))
                free("23", (state_done, 4))
                update(0, aux01)
                update(1, aux23).then_inc(upd_full, 1)

            def gla_update2():
                free("01", (state_done, 8))
                update(2, aux01).then_inc(upd_full, 1)

            def gla_out(m):
                dst, half = ((aux23, "23"), (aux01, "01"))[m]
                if m == 0:
                    pe.wait_ge(state_done, 4)
                free(half, (og_sq, 4 * m + 4), (yg_done, 1))
                for h in range(GH):
                    e = slice(GDV * h, GDV * h + GDV)
                    o = fours(dst)[:, h, :]
                    mm = pe.matmul(o, gla_at[:, 2 * h + m, :], gla_v[:, m, e], start=True, stop=False,
                                   skip_group_check=True)
                    for c in (2 * m, 2 * m + 1):
                        if c:
                            rows = slice(CH * (c % 2), CH * (c % 2) + CH)
                            mm = pe.matmul(o[rows, :], gla_q[:, h, CH * c:CH * c + CH], states[:, c - 1, h, :],
                                           start=False, stop=True, skip_group_check=True)
                mm.then_inc(og_full, 1)

            def qk_turn(q, dst):
                pe.wait_ge(roped, q + 1)
                free("01", (qk_copied, q + 1))
                for h in range(4):
                    for m in range(M):
                        mm = pe.transpose(fours(aux01)[:, h, P * m:P * m + P], z1[:, m, HD * h:HD * h + HD], ident[:])
                mm.then_inc(qk_full, 1)

            def ret_scores(h):
                pe.wait_ge(qk_copied, 6 + 2 * h)
                pe.wait_ge(acc_free, G_W2 + 9 + 4 * h)
                free("01", (s_decayed, 2 * h + 2))
                free("23", (s_state, h + 1))
                for n in range(4):
                    for m in range(M):
                        c = slice(P * m, P * m + P)
                        pe.matmul(fours(aux01)[:, n, c], half_k[h][:, n, c], half_q[h][:, n, c], start=True,
                                  stop=True, skip_group_check=True)
                    c = slice(HD * n, HD * n + HD)
                    mm = pe.matmul(aux[:, 2, c], k_dec[h][:, c], ret_v[h][:, 0, c], start=True, stop=True,
                                   skip_group_check=True)
                mm.then_inc(s_full, 1)

            def ret_out(h):
                pe.wait_ge(s_decayed, 2 * h + 2)
                free("23", (og_sq, 9 + h), (yg_done, 2 + h))
                for n in range(4):
                    c = slice(HD * n, HD * n + HD)
                    pe.matmul(aux[:, 2, c], half_k[h][:, n, 0:P], ret_v[h][:, 0, c], start=True, stop=True,
                              skip_group_check=True)
                    pe.matmul(aux[:, 3, c], half_k[h][:, n, P:T], ret_v[h][:, 1, c], start=True, stop=False,
                              skip_group_check=True)
                    mm = pe.matmul(aux[:, 3, c], half_q[h][:, n, P:T], k_dec[h][:, c], start=False, stop=True,
                                   skip_group_check=True)
                mm.then_inc(ret_full, 1)

            def ffn(b):
                f = FFN[b]
                u0, g0 = f["u"], f["g"]
                turn0 = (6, 21)[b]

                def part(act_b, k0, u, g, flipped, first, last):
                    for k in range(KU):
                        mm = products(act_b, k0 + k, k, u, flipped, g % 2, N, first and k == 0,
                                      last and k == KU - 1)
                    return mm

                def run(u, kind, q, g, step, i=None, tile=0):
                    down = kind == "down"
                    if down and q == 0:
                        pe.wait_ge(f_done, step + (f["it0"] + 1))
                    if down or q == 0:
                        pe.wait_ge(acc_free, g - 1 if i is None else i * 6 + (g - 1))
                    pe.wait_ge(lo_done, u + 1 if i is None else i * 12 + (u + 1))
                    if down:
                        mm = part(f["f_act"], tile, u, g, False, True, True)
                    else:
                        mm = part(f["act"], KU * q, u, g, True, q == 0, q == 3)
                    mm.then_inc(unit_used, 1)

                for n, (kind, q, step) in enumerate(FFN_HEAD):
                    if n < 4:
                        pe.wait_ge(turned, turn0 + q + 1)
                    run(u0 + n, kind, q, g0 + n // 4, step)
                    for name, *args in after.get(u0 + n, ()):
                        if name in tasks:
                            tasks[name](*args)
                with pe.Fori(0, ROUNDS) as i:
                    for n, (kind, q, ahead) in enumerate(FFN_ROUND):
                        g = g0 + 2 + {"gate": 0, "down": 1 + q, "value": 5}[kind]
                        run(u0 + 8 + n, kind, q, g, i + ahead if ahead else i, i)
                for n, (kind, q, step) in enumerate(FFN_TAIL):
                    u = u0 + FT_TAIL + n
                    g = g0 + G_TAIL + (n // 4 if n < 8 else n - 6)
                    run(u, kind, q, g, step, tile=KU if n >= 12 else 0)
                    for name, *args in after.get(u, ()):
                        if name in tasks:
                            tasks[name](*args)

            tasks = dict(turn=turn, norm_row=norm_row, tables=tables, scores=scores, probs_turn=probs_turn, weigh=weigh,
                         gate_logits=gate_logits, gate_sums=gate_sums, gla_scores=gla_scores,
                         gla_update01=gla_update01, gla_update2=gla_update2, gla_out0=lambda: gla_out(0),
                         gla_out1=lambda: gla_out(1), qk_turn=qk_turn, ret_scores=ret_scores, ret_out=ret_out)
            pe.wait_ge(const_in, 16)
            pe.wait_ge(mix_in, 16)
            pe.transpose(aux[:, 2, 0:DK], vec_rows[0:DK, :], ident[0:DK, 0:DK]).then_inc(cols_full, 1)
            walk(lambda u: multiply(u) if u >= 0 else None, tasks, -SPL - 1, F1)
            ffn(0)
            walk(multiply, tasks, PL1, F2)
            ffn(1)
            walk(multiply, tasks, PL2, UNITS)

        @block.gpsimd
        def _(pool):
            def rsqrt(dst, src, width, done):
                pool.tensor_tensor(dst, src, half_neg[:, 0:width], ALU.pow).then_inc(done, 1)

            def norm_factor(mean_count):
                pool.wait_ge(mean_done, mean_count)
                rsqrt(r_col, mean1, M, r_done)

            def head_factor(count):
                pool.wait_ge(z_sum, count)
                rsqrt(rr, ssh, 8, z_r)

            pool.wait_ge(x_in[NG - 1], 16)
            pool.dma_start(cumsum_m, a["c_cumsum"]).then_inc(gla_in, 16)
            pool.dma_start(chunk_mask.bitcast(U32), a["c_chunk_mask"]).then_inc(gla_in, 16)
            pool.dma_start(w_row[:], a["gla_norm_w"][0].partition_broadcast(P)).then_inc(gla_in, 16)
            pool.wait_ge(ones_done, 1)
            norm_factor(1)
            pool.dma_start(up_aug[0:RANK, :], a["w_gla_gate_up"][0]).then_inc(small_in, 16)
            pool.dma_start(up_aug[RANK:RANK + 1, :], a["b_gla_gate"]).then_inc(small_in, 16)
            rel = a["att_rel_bias"]
            for p in range(8):
                if p >= 2:
                    pool.wait_ge(biased, 2 * (p - 2) + 2)
                src = bass.AP(tensor=rel.tensor, offset=2 * p * (2 * REL + 1) + REL - P + 1,
                              ap=[[1, P], [2 * REL + 1, 2], [1, T]])
                pool.dma_start(bias[p % 2], src).then_inc(bias_in[p % 2], 16)
            head_factor(1)
            pool.wait_ge(turn_full, 6)
            pool.dma_start(x_sb, x_dram).then_inc(x_back, 16)
            pool.dma_start(p_sb, a["p"][0, 0].rearrange("(m p) n -> p m n", p=P)).then_inc(ple_in[0], 16)
            pool.dma_start(wf_b, a["final_norm_w"].partition_broadcast(P)).then_inc(ple_tab[0], 16)
            norm_factor(2)
            norm_factor(3)
            pool.wait_ge(x_fresh, 1)
            pool.dma_start(rope[0], a["c_rope_a"]).then_inc(tab_in, 16)
            pool.dma_start(rope[2], a["c_rope_r"]).then_inc(tab_in, 16)
            pool.dma_start(w_row[:, 0:HD], a["q_norm_2"][0].partition_broadcast(P)).then_inc(tab_in, 16)
            pool.dma_start(w_row[:, HD:2 * HD], a["k_norm_2"][0].partition_broadcast(P)).then_inc(tab_in, 16)
            pool.dma_start(k_decay, a["c_k_decay"]).then_inc(tab_in, 16)
            pool.dma_start(causal[:], a["c_causal"]).then_inc(tab_in, 16)
            for n in range(NG):
                pool.wait_ge(x_fresh, 2 * n + 2)
                pool.dma_start(spill[:, :, N * n:N * n + N], xc(n)).then_inc(x_stored, 16)
            pool.wait_ge(mean_done, 4)
            rsqrt(r_final, mean1, M, pool_step)
            pool.wait_ge(mean_done, 5)
            rsqrt(r_col, mean2, M, r_done)
            for q in range(4):
                head_factor(2 + q)

            def ret_tables(h):
                pool.dma_start(decay_m, a["c_decay"][:, 4 * h:4 * h + 4, :]).then_inc(ret_tab_in, 16)
                pool.dma_start(q_decay.rearrange("p a b -> p (a b)"),
                               a["c_q_decay"][0, N * h:N * h + N].partition_broadcast(P)).then_inc(ret_tab_in, 16)
                pool.dma_start(g_ret, a["g_ret_2"][0, N * h:N * h + N].partition_broadcast(P)).then_inc(ret_tab_in, 16)

            pool.wait_ge(o_done, 12)
            ret_tables(0)
            head_factor(6)
            pool.wait_ge(yg_done, 2)
            ret_tables(1)
            head_factor(7)
            pool.wait_ge(turn_full, 21)
            pool.wait_ge(x_stored, 16 * NG)
            pool.dma_start(x_sb, spill).then_inc(x_back, 16)
            pool.dma_start(p_sb, a["p_2"][0, 0].rearrange("(m p) n -> p m n", p=P)).then_inc(ple_in[1], 16)
            pool.dma_start(wf_b, a["b_ple_gate_2"][0].partition_broadcast(P)).then_inc(ple_tab[1], 16)
            norm_factor(6)
            norm_factor(7)
            for n in range(NG):
                pool.wait_ge(x_fresh, 2 * NG + n + 1)
                pool.dma_start(out_dram[:, :, N * n:N * n + N], xc(n)).then_inc(out_stored, 16)


_INS = ["x", "p", "norm_mix_w", "w_in", "att_rel_bias", "w_gla_gate_up", "b_gla_gate", "gla_norm_w", "w_out",
        "norm_ffn_w", "w_ffn_up", "w_ffn_conv", "b_ffn_conv", "w_ffn_down", "norm_ple_w", "w_ple_gate",
        "w_ple_proj", "final_norm_w", "p_2", "g_mix_2", "w_in_2", "q_norm_2", "k_norm_2", "g_ret_2", "w_o_2",
        "g_ffn_2", "w_gate_2", "w_up_2", "w_down_2", "g_ple_2", "w_ple_gate_2", "b_ple_gate_2", "w_ple_proj_2"]


def kernel(**inputs):
    import concourse.bacc as _bacc
    from concourse.bass_utils import run_bass_kernel_spmd as _run

    nc = _bacc.Bacc("TRN2", target_bir_lowering=False, num_devices=1)
    arrays, views = {}, {}
    for name in _INS:
        arr = np.ascontiguousarray(inputs[name])
        arrays[f"in_{name}"] = arr
        views[name] = nc.dram_tensor(f"in_{name}", arr.shape, mybir.dt.from_np(arr.dtype), kind="ExternalInput").ap()
    for name, arr in shape_constants().items():
        arrays[name] = arr
        views[name] = nc.dram_tensor(name, arr.shape, mybir.dt.from_np(arr.dtype), kind="ExternalInput").ap()
    out = nc.dram_tensor("out", (1, T, D), F32, kind="ExternalOutput").ap()
    x_spill = nc.dram_tensor("x_spill", (T, D), F32, kind="Internal").ap()
    build_two_blocks(nc, views, out, x_spill)
    r = _run(nc, [arrays], core_ids=[0])
    return r.results[0]["out"]
```
